# Optimizing a Trainium2 kernel written in Bass

```python
import jax, jax.numpy as jnp
from jax import lax
import numpy as np

D_MODEL = 1024
BATCH = 1
SEQ = 256
DEPTH = 1

GRID_W = 64
CTX_LEN = 256
EPS = 1e-6

RET_HEADS = 4
RET_QK_DIM = 256
RET_V_DIM = 512
RET_CHUNK = 128
ATTN_HEADS = 8
ATTN_KV_HEADS = 2
ATTN_HEAD_DIM = 128
Q_BLOCK = 128
ROPE_THETA = 10000.0
N_EXPERTS = 32
TOP_K = 4
EXPERT_FF = 1024
SWIGLU_LIMIT = 7.0
SWIGLU_ALPHA = 1.702

RET_QK_W = RET_HEADS * RET_QK_DIM
RET_V_W = RET_HEADS * RET_V_DIM
ATTN_Q_W = ATTN_HEADS * ATTN_HEAD_DIM
ATTN_KV_W = ATTN_KV_HEADS * ATTN_HEAD_DIM
IN_SIZES = (RET_QK_W, RET_QK_W, RET_V_W, RET_V_W, ATTN_Q_W, ATTN_KV_W, ATTN_KV_W, D_MODEL, D_MODEL)
IN_WIDTH = sum(IN_SIZES)

kernel_name = 'hybrid_retention_gqa_moe_diffusion_block'

def rms_norm(x, gain=None):
    xf = x.astype(jnp.float32)
    y = xf * lax.rsqrt(jnp.mean(xf * xf, axis=-1, keepdims=True) + EPS)
    if gain is not None:
        y = y * gain.astype(jnp.float32)
    return y.astype(x.dtype)

def modulate(x, gain, shift, scale):
    return rms_norm(x, gain) * (1 + scale) + shift

def split_in_proj(p):
    idx = np.cumsum(IN_SIZES)[:-1].tolist()
    return jnp.split(p, idx, axis=-1)

def split_heads(t, n_heads):
    b, l, w = t.shape
    return t.reshape(b, l, n_heads, w // n_heads).transpose(0, 2, 1, 3)

def merge_heads(t):
    b, n, l, d = t.shape
    return t.transpose(0, 2, 1, 3).reshape(b, l, n * d)

def axial_rope(rows, head_dim):
    row_id = jnp.broadcast_to(jnp.arange(rows, dtype=jnp.float32)[:, None], (rows, GRID_W)).reshape(-1)
    col_id = jnp.broadcast_to(jnp.arange(GRID_W, dtype=jnp.float32)[None, :], (rows, GRID_W)).reshape(-1)
    n_freq = head_dim // 4
    inv_freq = ROPE_THETA ** (-jnp.arange(n_freq, dtype=jnp.float32) / n_freq)
    ang = jnp.stack([row_id[:, None] * inv_freq, col_id[:, None] * inv_freq], axis=1)
    return jnp.cos(ang), jnp.sin(ang)

def apply_rope(x, cos, sin):
    shp = x.shape
    xf = x.astype(jnp.float32).reshape(shp[:-1] + (2, 2, shp[-1] // 4))
    x1, x2 = xf[..., 0, :], xf[..., 1, :]
    o = jnp.stack([x1 * cos - x2 * sin, x2 * cos + x1 * sin], axis=-2)
    return o.reshape(shp).astype(x.dtype)

def retention_scan(q, k, v, log_gamma, s0, include_diag):
    b, h, l, dk = q.shape
    dv = v.shape[-1]
    n_chunks = l // RET_CHUNK
    pos = jnp.arange(RET_CHUNK, dtype=jnp.float32)
    diff = pos[:, None] - pos[None, :]
    mask = (diff >= 0) if include_diag else (diff > 0)
    lg = log_gamma.astype(jnp.float32)
    d_intra = jnp.where(mask[None], jnp.exp(lg[:, None, None] * jnp.maximum(diff, 0.0)[None]), 0.0)
    d_in = jnp.exp(lg[:, None] * (pos + 1.0))[None, :, :, None]
    d_out = jnp.exp(lg[:, None] * (RET_CHUNK - 1.0 - pos))[None, :, :, None]
    d_chunk = jnp.exp(lg * RET_CHUNK)[None, :, None, None]

    def to_chunks(t):
        return t.reshape(b, h, n_chunks, RET_CHUNK, t.shape[-1]).transpose(2, 0, 1, 3, 4)

    def step(s, xs):
        qc, kc, vc = (t.astype(jnp.float32) for t in xs)
        scores = jnp.einsum('bhid,bhjd->bhij', qc, kc) * d_intra
        o = jnp.einsum('bhij,bhje->bhie', scores, vc) + jnp.einsum('bhid,bhde->bhie', qc, s) * d_in
        s = s * d_chunk + jnp.einsum('bhjd,bhje->bhde', kc * d_out, vc)
        return s, o

    s_fin, o = lax.scan(step, s0, (to_chunks(q), to_chunks(k), to_chunks(v)))
    o = o.transpose(1, 2, 0, 3, 4).reshape(b, h, l, dv).astype(v.dtype)
    return o, s_fin

def bidir_retention(q, k, v, lg_f, lg_b, s_f0, s_b0):
    o_f, s_f = retention_scan(q, k, v, lg_f, s_f0, True)
    o_b, s_b = retention_scan(jnp.flip(q, 2), jnp.flip(k, 2), jnp.flip(v, 2), lg_b, s_b0, False)
    return o_f + jnp.flip(o_b, 2), s_f, s_b

def block_attention(q, k, v):
    b, kvh, g, lq, d = q.shape
    n_blk = lq // Q_BLOCK
    qb = jnp.moveaxis(q.reshape(b, kvh, g, n_blk, Q_BLOCK, d), 3, 0)
    scale = d ** -0.5

    def one_block(q_blk):
        s = jnp.einsum('bkgqd,bksd->bkgqs', q_blk, k, preferred_element_type=jnp.float32) * scale
        p = jax.nn.softmax(s, axis=-1)
        return jnp.einsum('bkgqs,bksd->bkgqd', p.astype(v.dtype), v,
                          preferred_element_type=jnp.float32).astype(v.dtype)

    o = lax.map(one_block, qb)
    return jnp.moveaxis(o, 0, 3).reshape(b, kvh * g, lq, d)

def group_q(t):
    b, h, l, d = t.shape
    return t.reshape(b, ATTN_KV_HEADS, h // ATTN_KV_HEADS, l, d)

def merge_branches(ret_o, ret_g, attn_o, gate_r, gate_a, w_ret_o, w_attn_o, w_out):
    ret_branch = (jax.nn.silu(ret_g) * merge_heads(rms_norm(ret_o))) @ w_ret_o
    attn_branch = merge_heads(attn_o) @ w_attn_o
    y = jax.nn.sigmoid(gate_r) * ret_branch + jax.nn.sigmoid(gate_a) * attn_branch
    return y @ w_out

def moe(h, w_router, b_router, w1, b1, w2, b2):
    shp = h.shape
    t = h.reshape(-1, shp[-1])
    logits = (t @ w_router).astype(jnp.float32) + b_router.astype(jnp.float32)
    top_v, top_i = lax.top_k(logits, TOP_K)
    wts = jax.nn.softmax(top_v, axis=-1)
    comb = jnp.sum(jax.nn.one_hot(top_i, N_EXPERTS, dtype=jnp.float32) * wts[..., None], axis=1)

    def expert(acc, xs):
        w1e, b1e, w2e, b2e, ce = xs
        a = t @ w1e + b1e
        gate = jnp.minimum(a[:, :EXPERT_FF], SWIGLU_LIMIT)
        up = jnp.clip(a[:, EXPERT_FF:], -SWIGLU_LIMIT, SWIGLU_LIMIT)
        out = (gate * jax.nn.sigmoid(SWIGLU_ALPHA * gate) * (up + 1)) @ w2e + b2e
        return acc + ce[:, None].astype(out.dtype) * out, None

    out, _ = lax.scan(expert, jnp.zeros_like(t), (w1, b1, w2, b2, comb.T))
    return out.reshape(shp)

def setup_inputs(seed: int = 0) -> dict:
    key = jax.random.key(seed)
    ks = jax.random.split(key, 24)
    f32 = jnp.float32

    def nrm(k, shape, scale):
        return jax.random.normal(k, shape, f32) * scale

    base = -np.log1p(-2.0 ** (-5.0 - np.arange(RET_HEADS)))
    raw = jnp.asarray(np.log(np.expm1(base)).astype(np.float32))
    return {
        'x': nrm(ks[0], (BATCH, SEQ, D_MODEL), 1.0),
        'c': nrm(ks[1], (BATCH, D_MODEL), 1.0),
        'ctx': nrm(ks[2], (BATCH, CTX_LEN, D_MODEL), 1.0),
        'c_ctx': nrm(ks[3], (D_MODEL,), 1.0),
        'norm1': 1.0 + nrm(ks[4], (DEPTH, D_MODEL), 0.01),
        'norm2': 1.0 + nrm(ks[5], (DEPTH, D_MODEL), 0.01),
        'w_ada': nrm(ks[6], (DEPTH, D_MODEL, 6 * D_MODEL), 0.5 * D_MODEL ** -0.5),
        'b_ada': nrm(ks[7], (DEPTH, 6 * D_MODEL), 0.01),
        'w_in': nrm(ks[8], (DEPTH, D_MODEL, IN_WIDTH), D_MODEL ** -0.5),
        'ret_decay_f': raw + nrm(ks[9], (DEPTH, RET_HEADS), 0.05),
        'ret_decay_b': raw + nrm(ks[10], (DEPTH, RET_HEADS), 0.05),
        'attn_q_norm': 1.0 + nrm(ks[11], (DEPTH, ATTN_HEAD_DIM), 0.01),
        'attn_k_norm': 1.0 + nrm(ks[12], (DEPTH, ATTN_HEAD_DIM), 0.01),
        'w_ret_o': nrm(ks[13], (DEPTH, RET_V_W, D_MODEL), RET_V_W ** -0.5),
        'w_attn_o': nrm(ks[14], (DEPTH, ATTN_Q_W, D_MODEL), ATTN_Q_W ** -0.5),
        'w_out': nrm(ks[15], (DEPTH, D_MODEL, D_MODEL), D_MODEL ** -0.5),
        'w_router': nrm(ks[16], (DEPTH, D_MODEL, N_EXPERTS), D_MODEL ** -0.5),
        'b_router': nrm(ks[17], (DEPTH, N_EXPERTS), 0.01),
        'w_exp_in': nrm(ks[18], (DEPTH, N_EXPERTS, D_MODEL, 2 * EXPERT_FF), D_MODEL ** -0.5),
        'b_exp_in': nrm(ks[19], (DEPTH, N_EXPERTS, 2 * EXPERT_FF), 0.01),
        'w_exp_out': nrm(ks[20], (DEPTH, N_EXPERTS, EXPERT_FF, D_MODEL), EXPERT_FF ** -0.5),
        'b_exp_out': nrm(ks[21], (DEPTH, N_EXPERTS, D_MODEL), 0.01),
    }

def reference(x, c, ctx, c_ctx, norm1, norm2, w_ada, b_ada, w_in, ret_decay_f, ret_decay_b,
              attn_q_norm, attn_k_norm, w_ret_o, w_attn_o, w_out, w_router, b_router,
              w_exp_in, b_exp_in, w_exp_out, b_exp_out):
    b = x.shape[0]
    rows = x.shape[1] // GRID_W
    rope_ret = axial_rope(rows, RET_QK_DIM)
    rope_attn = axial_rope(rows, ATTN_HEAD_DIM)
    k_scale = RET_QK_DIM ** -0.5
    zero_state = jnp.zeros((b, RET_HEADS, RET_QK_DIM, RET_V_DIM), jnp.float32)

    for i in range(DEPTH):
        mod = jax.nn.silu(c) @ w_ada[i] + b_ada[i]
        mod_c = jax.nn.silu(c_ctx) @ w_ada[i] + b_ada[i]
        sh1, sc1, g1, sh2, sc2, g2 = jnp.split(mod[:, None, :], 6, axis=-1)
        sh1c, sc1c, g1c, sh2c, sc2c, g2c = jnp.split(mod_c, 6, axis=-1)

        h = modulate(x, norm1[i], sh1, sc1)
        hc = modulate(ctx, norm1[i], sh1c, sc1c)
        qr, kr, vr, gr, qa, ka, va, gate_r, gate_a = split_in_proj(h @ w_in[i])
        qrc, krc, vrc, grc, qac, kac, vac, gate_rc, gate_ac = split_in_proj(hc @ w_in[i])

        lg_f = -jax.nn.softplus(ret_decay_f[i].astype(jnp.float32))
        lg_b = -jax.nn.softplus(ret_decay_b[i].astype(jnp.float32))
        o_rc, s_f, s_b = bidir_retention(split_heads(qrc, RET_HEADS), split_heads(krc, RET_HEADS) * k_scale,
                                         split_heads(vrc, RET_HEADS), lg_f, lg_b, zero_state, zero_state)
        q_r = apply_rope(split_heads(qr, RET_HEADS), *rope_ret)
        k_r = apply_rope(split_heads(kr, RET_HEADS), *rope_ret) * k_scale
        o_r, _, _ = bidir_retention(q_r, k_r, split_heads(vr, RET_HEADS), lg_f, lg_b, s_f, s_b)

        k_ac = rms_norm(split_heads(kac, ATTN_KV_HEADS), attn_k_norm[i])
        v_ac = split_heads(vac, ATTN_KV_HEADS)
        q_a = apply_rope(rms_norm(split_heads(qa, ATTN_HEADS), attn_q_norm[i]), *rope_attn)
        k_a = apply_rope(rms_norm(split_heads(ka, ATTN_KV_HEADS), attn_k_norm[i]), *rope_attn)
        v_a = split_heads(va, ATTN_KV_HEADS)
        o_a = block_attention(group_q(q_a), jnp.concatenate([k_ac, k_a], axis=2),
                              jnp.concatenate([v_ac, v_a], axis=2))

        x = x + g1 * merge_branches(o_r, gr, o_a, gate_r, gate_a, w_ret_o[i], w_attn_o[i], w_out[i])

        if i + 1 < DEPTH:
            q_ac = rms_norm(split_heads(qac, ATTN_HEADS), attn_q_norm[i])
            o_ac = block_attention(group_q(q_ac), k_ac, v_ac)
            ctx = ctx + g1c * merge_branches(o_rc, grc, o_ac, gate_rc, gate_ac, w_ret_o[i], w_attn_o[i], w_out[i])
            ctx = ctx + g2c * moe(modulate(ctx, norm2[i], sh2c, sc2c), w_router[i], b_router[i],
                                  w_exp_in[i], b_exp_in[i], w_exp_out[i], b_exp_out[i])

        x = x + g2 * moe(modulate(x, norm2[i], sh2, sc2), w_router[i], b_router[i],
                         w_exp_in[i], b_exp_in[i], w_exp_out[i], b_exp_out[i])
    return x


_drawn_inputs = setup_inputs


def setup_inputs(seed=0):
    import zlib

    import numpy as np

    out = dict(_drawn_inputs(seed))
    spreads = {}
    factors = {'norm1': 7.471,
     'norm2': 3.955,
     'b_ada': 3.001,
     'attn_q_norm': 8.0,
     'attn_k_norm': 8.0,
     'b_router': 21.897,
     'b_exp_in': 21.419,
     'b_exp_out': 64.0}
    for name, (base, spread) in spreads.items():
        noise = np.random.default_rng([zlib.crc32(name.encode()), seed]).standard_normal(out[name].shape)
        drawn = base * np.exp(spread * noise) if base else spread * noise
        out[name] = __import__('jax').numpy.asarray(drawn.astype(out[name].dtype))
    for name, factor in factors.items():
        out[name] = (out[name] * factor).astype(out[name].dtype)
    return out
```

```python
import concourse.bass as bass
from concourse import mybir
from contextlib import ExitStack, contextmanager

P = 128
D = 1024
KB = D // P
SEQ = 256
CTX = 256
RH, RQK, RV = 4, 256, 512
AH, AKV, AD = 8, 2, 128
E, FF, TOPK = 32, 1024, 4
CAP = 64
CW = 512
EPS = 1e-6
LIMIT, ALPHA = 7.0, 1.702
KIB = 256

IN_COLS = {"qr": 0, "kr": 1024, "vr": 2048, "gr": 4096, "qa": 6144, "ka": 7168, "gate_r": 7680, "gate_a": 8704}

C_ID, C_ID2, C_SLOT, C_TRI, C_DIST, C_SEL = 0, 128, 192, 320, 448, 960
C_ROPER = C_SEL + 256
C_ROPEA = C_ROPER + 1024
C_END = C_ROPEA + 512


def chunks():
    out = [("ada", c, 0, c * CW) for c in range(4)]

    def w_in(kind, c):
        return (kind, c, 0, IN_COLS[kind] + c * CW)

    out += [w_in("qa", 0), w_in("qa", 1), w_in("ka", 0)]
    for pair in range(2):
        out += [w_in("qr", pair), w_in("kr", pair)]
        for h in (2 * pair, 2 * pair + 1):
            out += [w_in("vr", h), w_in("gr", h)]
    out += [w_in("gate_r", 0), w_in("gate_r", 1), w_in("gate_a", 0), w_in("gate_a", 1)]
    out += [("ada", c, 0, c * CW) for c in range(4, 8)]
    out += [("ret_o", 2 * col + kh, kh * D, col * CW) for col in range(2) for kh in range(2)]
    out += [("ada", c, 0, c * CW) for c in range(8, 12)]
    out += [("attn_o", c, 0, c * CW) for c in range(2)]
    out += [("out", c, 0, c * CW) for c in range(2)]
    return out


CHUNKS = chunks()
NPRE = 2 * len(CHUNKS)
CHUNK_OF = {c[:2]: n for n, c in enumerate(CHUNKS)}
TILES_OF = {"qr": (2, 3), "kr": (0, 1, 2, 3), "vr": (0, 1, 2, 3), "gr": (2, 3), "qa": (2, 3),
            "ka": (0, 1, 2, 3), "gate_r": (2, 3), "gate_a": (2, 3)}


def psum_plan():
    plan = [(("xT", k), "dve") for k in range(KB)]
    plan += [(("ada", c), "act") for c in range(4)] + [(("cols",), "dve")]
    reader = {"qr": "dve", "kr": "dve", "vr": "act", "gr": "dve", "qa": "act", "ka": "act",
              "gate_r": "act", "gate_a": "act"}
    after = {}
    s = 0
    slots = []
    for kind, c, _, _ in CHUNKS:
        if kind in reader:
            for t in TILES_OF[kind]:
                slots.append((kind, c, t))
                if kind in ("qa", "ka", "qr", "kr"):
                    after.setdefault(s + 1, []).append((("rT", kind, c, t), "act"))
                s += 1

    def at(n, name, who):
        after.setdefault(n, []).append((name, who))

    first = slots.index(("qr", 0, 2)) + 1
    for u in range(2 * AH):
        n = first + 2 * u // 3
        at(n, ("score", u // 2, u % 2), "act")
        at(n + 1, ("pT", u // 2, u % 2), "act")
        if u % 2:
            at(n + 2, ("av", u // 2), "dve")
    done = {}
    for h in range(RH):
        v_end, g_end = slots.index(("vr", h, 3)), slots.index(("gr", h, 3))
        at(v_end, ("rs", h, 0), "dve")
        at(v_end, ("rs", h, 1), "dve")
        at(g_end, ("ro", h, 0), "dve")
        at(g_end, ("ro", h, 1), "dve")
        at(g_end + (4 if h == 0 else 3), ("oT", h, 0), "act")
        at(g_end + (4 if h == 0 else 3), ("oT", h, 1), "act")
    for n, (kind, c, t) in enumerate(slots):
        plan.append((("proj", kind, c, t), reader[kind]))
        order = {"av": 0, "pT": 1, "rT": 2, "score": 3}
        plan += sorted(after.get(n, []), key=lambda x: order.get(x[0][0], 4))
    plan += [(("ada", c), "act") for c in range(4, 8)]
    plan += [(("b1", 0), "act")]
    plan += [(("ret_o", col, t), "dve") for col in range(2) for t in (2, 3)]
    plan += [(("ada", c), "act") for c in range(8, 12)]
    plan += [(("attn_o", c, t), "dve") for c in range(2) for t in (2, 3)]
    plan += [(("yT", j), "dve") for j in range(4)]
    plan += [(("bc", j), "act") for j in (0, 1, 2, 3, 4, 5)]
    plan += [(("out", c, t), "dve") for c in range(2) for t in (2, 3)]
    plan += [(("bc", j), "act") for j in (6, 7)]
    plan += [(("h2T", j), "act") for j in range(4)]
    plan += [(("logits",), "dve"), (("rank",), "dve"), (("combT",), "dve")]
    return plan


PLAN = psum_plan()
TILE_AT = {name: n for n, (name, _) in enumerate(PLAN)}
READ_AT = {}
for _n, (_name, _who) in enumerate(PLAN):
    READ_AT[_name] = 1 + sum(w == _who for _, w in PLAN[:_n])


def hybrid_block(nc, x, ctx_in, norm2, w_ada, b_ada, w_in, decay_f, decay_b, q_norm,
                 k_norm, w_ret_o, w_attn_o, w_out, w_router, b_router, w1, b1, w2, b2, vectors, consts, out):
    f32, f32r = mybir.dt.float32, mybir.dt.float32r
    ALU, ACT, AX = mybir.AluOpType, mybir.ActivationFunctionType, mybir.AxisListType
    stack = ExitStack()
    with stack:
        base = -(-nc.sbuf_base // 32) * 32
        size = (nc.sbuf_usable_end - base) // 4 // 8 * 8
        stack.enter_context(nc.sbuf_tensor("slab", [P, (nc.sbuf_usable_end - base) // 4 - 8], f32))

        def at(name, kib, shape, dtype=f32, extra=0):
            n = 1
            for s in shape[1:]:
                n *= s
            assert kib * 1024 + extra + 4 * n <= 4 * size, name
            return nc.alloc_sbuf_tensor_at(name, shape, dtype, offset=base + int(kib * 1024) + extra)

        raw = [at(f"raw{s}", 8 * s, [P, 4, CW]) for s in range(8)]
        wl = [at(f"wl{s}", 8 * s, [P, 4, CW], f32r) for s in range(8)]
        wh = [at(f"wh{s}", 64 + 8 * s, [P, 4, CW], f32r) for s in range(4)]
        hH = at("hH", 96, [P, KB, 512], f32r)
        hL = at("hL", 112, [P, KB, 512], f32r)
        silu_c = at("silu_c", 128, [P, KB, P], f32r)
        F = 132
        rows = at("rows", F, [P, 4, D])
        xT = at("xT", F + 16, [P, KB, 512])
        mod1 = at("mod1", F + 32, [5, 2048])
        qaT = at("qaT", F, [P, AH, SEQ])
        kaT = at("kaT", F + 8, [P, AKV, 512])
        va = at("va", F + 12, [P, 4, AKV * AD])
        prob = [at(f"prob{s}", F + 16 + 2 * s, [P, 512]) for s in range(2)]
        probT = at("probT", F + 20, [P, 4, SEQ])
        oaT = at("oaT", F + 24, [P, AH, SEQ])
        oT = at("oT", F, [P, RH * 4, SEQ])
        qrT = at("qrT", F + 32, [P, 4, SEQ])
        krT = at("krT", F + 36, [P, 4, 512])
        v = at("v", F + 44, [P, 4, RV])
        g = at("g", F + 52, [P, 2, RV])
        decay = at("decay", F + 56, [P, 4, SEQ])
        decay2 = at("decay2", F + 60, [P, 512])
        roped = [at(f"roped{s}", F + 62 + 2 * s, [P, 512]) for s in range(2)]
        ropes = at("ropes", F + 66, [P, 512])
        rope_r = at("rope_r", F + 68, [P, 2, 2, 256])
        rope_a = at("rope_a", F + 56, [P, 2, 2, 128])
        gains = at("gains", F + 58, [P, 2, 128])
        dist = at("dist", F + 72, [P, 2, SEQ])
        gate_r = at("gate_r", F + 32, [P, 2, D])
        gate_a = at("gate_a", F + 40, [P, 2, D])
        mod2 = at("mod2", F + 48, [5, 4096])
        oH = at("oH", 96, [P, RH * 4, SEQ], f32r)
        oL = at("oL", 112, [P, RH * 4, SEQ], f32r)
        aH = at("aH", F, [P, AH, SEQ], f32r)
        aL = at("aL", F + 8, [P, AH, SEQ], f32r)
        yH = at("yH", F + 16, [P, KB, SEQ], f32r)
        yL = at("yL", F + 24, [P, KB, SEQ], f32r)
        x1 = at("x1", F + 64, [P, 2, D])
        bc = at("bc", F + 32, [P, 4, D])
        norm2_b = at("norm2_b", 124, [P, D])
        h2 = at("h2", F, [P, 2, D])
        h2T = at("h2T", F + 8, [P, KB, SEQ])
        for s, kib in enumerate((F + 24, F + 32, F + 48, F + 56)):
            raw.append(at(f"raw{8 + s}", kib, [P, 4, CW]))
            wl.append(at(f"wl{8 + s}", kib, [P, 4, CW], f32r))
        h2H = at("h2H", 96, [P, 2, D], f32r)
        h2L = at("h2L", 104, [P, 2, D], f32r)
        xg = at("xg", 112, [P, KB, P], f32r)
        b2_sb = at("b2_sb", 112, [E, D])
        act_hl = at("act_hl", 116, [P, KB, P], f32r)
        wr_sb = at("wr_sb", 116, [P, KB, E])
        onehot = at("onehot", 120, [P, 2, CAP], f32r)
        ident2 = at("ident2", 120, [P, CAP], extra=512)
        slot_no = at("slot_no", 120, [P, P], extra=768)
        tri = at("tri", 120, [P, P], extra=1280)
        ones = at("ones", 120, [P, P], extra=1792)
        br_b = at("br_b", 120, [P, E], extra=2304)
        a_sb = at("a_sb", F, [P, 2 * FF])
        out2 = at("out2", F + 8, [P, D])
        gate = at("gate", F + 12, [P, 512])
        sig = at("sig", F + 14, [P, 512])
        up = at("up", F + 16, [P, 512])
        spread = at("spread", F + 18, [P, 2, P])
        spreadT = at("spreadT", F + 19, [P, SEQ])
        lp = at("lp", F + 20, [P, 2, 40])
        lm = at("lm", F + 20, [P, 2, 40], extra=320)
        top = at("top", F + 20, [P, 2, 8], extra=640)
        rep = at("rep", F + 20, [P, 2, 8], extra=704)
        chosen = at("chosen", F + 20, [P, 2, E], extra=768)
        comb = at("comb", F + 21, [P, 2, E])
        rank = at("rank", F + 21, [P, 2, E], extra=256)
        route = at("route", F + 21, [P, 16], extra=512)
        now_rank = at("now_rank", F + 21, [P, 2, 1], extra=576)
        own_rank = at("own_rank", F + 21, [P, 2, 1], extra=608)
        own_comb = at("own_comb", F + 21, [P, 2, 1], extra=640)
        most = at("most", F + 21, [P, 1], extra=672)
        most_int = at("most_int", F + 21, [P, 1], mybir.dt.int32, extra=704)
        combT = at("combT", F + 22, [E, SEQ])
        junk2 = at("junk2", F, [P, D])
        b1_rows = at("b1_rows", F + 16, [E, 2 * FF])
        b1_cols = at("b1_cols", F + 72, [P, 16, E])
        ident = at("ident", F + 74, [P, P])
        sel = at("sel", F + 74, [5, 2 + P], extra=512)
        stat = at("stat", F + 74, [P, 32], extra=1056)
        logdec = at("logdec", F + 74, [P, 2 * RH], extra=1184)
        lowdec = at("lowdec", F + 74, [P, 2 * RH], extra=1216)
        decin = at("decin", F + 74, [P, 2 * RH], extra=1248)
        cols_in = at("cols_in", F + 40, [P, 3, KB])
        cc = at("cc", F + 40, [P, KB, 2], extra=96)
        scale1 = at("scale1", F + 41, [P, KB, 2])
        shift1 = at("shift1", F + 41, [P, KB, 2], extra=64)

        banks = [stack.enter_context(nc.psum_tensor(f"bank{b}", [P, 512], f32)) for b in range(8)]

        def sem(name):
            return stack.enter_context(nc.semaphore(name))

        raw_in = [sem(f"raw_in{s}") for s in range(12)]
        first_half_used = sem("first_half_used")
        h_ready, l_ready = sem("high_half_ready"), sem("low_half_ready")
        psum_full = sem("psum_full")
        read = {"act": sem("psum_read_by_act"), "dve": sem("psum_read_by_dve")}
        half_k_used = sem("half_k_used")
        in_ident, in_rows, in_cols = sem("in_ident"), sem("in_rows"), sem("in_cols")
        in_tables, in_decay, in_bada = sem("in_tables"), sem("in_decay"), sem("in_b_ada")
        in_x1, in_mod2, in_b1, in_late = sem("in_x1"), sem("in_mod2"), sem("in_b1"), sem("in_late")
        in_norm2 = sem("in_norm2")
        squares = sem("squares_summed")
        var_ready, std_ready = sem("var_ready"), sem("std_ready")
        normed, silu_ready, sigm = sem("rows_normed"), sem("silu_c_ready"), sem("sigmoid_of_c")
        mods_ready, h_rounded, h_split = sem("mods_ready"), sem("h_rounded"), sem("h_split")
        h_full = sem("h_modulated")
        roped_ready, neg_max, prob_ready = sem("roped_ready"), sem("neg_max"), sem("prob_ready")
        exponent, exp_done, decay_ready = sem("exponent_ready"), sem("decay_exps"), sem("decay_ready")
        dec_abs, dec_ready = sem("softplus_parts"), sem("log_decay_ready")
        sg_ready = sem("sigmoid_g")
        oH_ready, oL_ready = sem("o_rounded"), sem("o_split")
        y_ready, yH_ready = sem("y_ready"), sem("y_rounded")
        x1_ready, h2_ready = sem("x1_ready"), sem("h2_ready")
        h2_rounded, h2_split = sem("h2_rounded"), sem("h2_split")
        expl, chosen_ready, comb_ready = sem("exp_logits"), sem("chosen_ready"), sem("comb_ready")
        neg_top, comb_t, rank_ready = sem("neg_top"), sem("combT_ready"), sem("rank_ready")
        g_full, a_read, o_read = sem("chunk_full"), sem("first_read"), sem("second_read")
        x_full, xg_ready = sem("gather_full"), sem("gather_read")
        onehot_ready, spread_ready = sem("onehot_ready"), sem("spread_ready")
        tp_full, tp_read = sem("spreadT_full"), sem("spreadT_read")
        t_full, t_read = sem("turned_full"), sem("turned_read")
        scattered = sem("scattered")
        clipped, sig_ready = sem("gate_clipped"), sem("sigmoid_gate")
        act_ready, act_high, act_low = sem("act_ready"), sem("act_high"), sem("act_low")
        most_ready = sem("most_tokens_ready")
        shifted, up_steps, columns_ready = sem("rank_shifted"), sem("up_steps"), sem("columns_ready")
        y_out, out_done = sem("y_out"), sem("out_done")
        chain = {n: sem(f"{n}_step") for n in ("act", "dve", "pool")}

        weights = {"ada": w_ada, "ret_o": w_ret_o, "attn_o": w_attn_o, "out": w_out}

        def half_source(n):
            kind, _, row, col = CHUNKS[n // 2]
            w = weights.get(kind, w_in)
            r = row + 512 * (n % 2)
            return w[0, r:r + 512, col:col + CW].rearrange("(k p) n -> p k n", p=P)

        FIRST_PASS = 0
        PLACES = (10, 11, 6, 7, 0, 1, 2, 3, 4, 5, 8, 9)
        assert NPRE % 8 == 6
        BEFORE = [sum(1 for n in range(NPRE) if n % 8 == s) for s in range(8)] + [0] * 4

        def raw_count(m):
            s = PLACES[m % 12]
            return s, 16 * (BEFORE[s] + m // 12 + 1)

        def chunk_released(n):
            kind, c, _, _ = CHUNKS[n]
            if kind == "ret_o":
                if c % 2 == 0:
                    return half_k_used, c // 2 + 1
                return psum_full, TILE_AT[("ret_o", c // 2, 3)] + 1
            if kind == "ada":
                return psum_full, TILE_AT[("ada", c)] + 1
            if kind in ("attn_o", "out"):
                return psum_full, TILE_AT[(kind, c, 3)] + 1
            return psum_full, TILE_AT[("proj", kind, c, 3)] + 1

        FIRST_TILE = {}
        for n_, (kind, c_, _, _) in enumerate(CHUNKS):
            if kind == "ada":
                FIRST_TILE.setdefault(TILE_AT[("ada", c_)], []).append(n_)
            elif kind == "ret_o":
                FIRST_TILE.setdefault(TILE_AT[("ret_o", c_ // 2, 2)], []).append(n_)
            elif kind in ("attn_o", "out"):
                FIRST_TILE.setdefault(TILE_AT[(kind, c_, 2)], []).append(n_)
            else:
                FIRST_TILE.setdefault(TILE_AT[("proj", kind, c_, TILES_OF[kind][0])], []).append(n_)

        def bank_of(name):
            return banks[TILE_AT[name] % 8]

        def full(eng, name):
            eng.wait_ge(psum_full, TILE_AT[name] + 1)

        def was_read(eng, name):
            eng.wait_ge(read[PLAN[TILE_AT[name]][1]], READ_AT[name])

        class Steps:

            def __init__(self, eng, which, start=0):
                self.eng, self.sem, self.n, self.add = eng, chain[which], start, 0

            def link(self, ins):
                self.n += 1
                ins.then_inc(self.sem, 1)
                self.eng.wait_ge(self.sem, self.add + self.n)

        ROPED = [x[0] for x in PLAN if x[0][0] == "rT"]

        def plain(r):
            return ROPED[r][1] == "kr" and ROPED[r][3] < 2

        def in_roped(eng, r):
            if plain(r):
                was_read(eng, ("proj",) + ROPED[r][1:])
            else:
                eng.wait_ge(roped_ready, sum(not plain(j) for j in range(r + 1)))


        def all_rounds(eng, round_, p=0):
            round_(0, p, 0, E * p)
            round_(1, p, 4, E * p)
            with eng.Fori(2, E - 1) as i:
                round_(i, p, 4, E * p + (i - 1))
            round_(E - 1, p, 4 + 6 * (E - 2), E * p)
            round_(E, p, 4 + 6 * (E - 1), E * p)

        def is_at(i, n):
            return isinstance(i, int) and i == n

        @contextmanager
        def more_passes(eng):
            eng.wait_ge(most_ready, 1)
            count = eng.value_load(most_int[0:1, 0:1], min_val=0, max_val=SEQ)
            with eng.If(count > CAP):
                with eng.Fori(1, SEQ // CAP) as p:
                    yield p

        block = stack.enter_context(nc.Block())

        @block.sync
        def _(sp):
            sp.dma_start(cols_in[:].rearrange("p a k -> p (a k)"), vectors).then_inc(in_cols, 16)
            sp.dma_start(rows[:, 2:4, :], x[0].rearrange("(t p) d -> p t d", p=P)).then_inc(in_rows, 16)
            sp.dma_start(rows[:, 0:2, :], ctx_in[0].rearrange("(t p) d -> p t d", p=P)).then_inc(in_rows, 16)
            sp.dma_start(ident[:], consts[:, C_ID:C_ID + P]).then_inc(in_ident, 16)
            sp.dma_start(sel[:], consts[0:5, C_SEL:C_SEL + 2 + P]).then_inc(in_ident, 16)
            sp.dma_start(mod1[4:5, :], b_ada[:, 0:2048]).then_inc(in_bada, 16)

            def load(n):
                if n >= 8:
                    sp.wait_ge(*chunk_released(n // 2 - 4))
                sp.dma_start(raw[n % 8][:], half_source(n)).then_inc(raw_in[n % 8], 16)

            for n in range(6):
                load(n)
            sp.dma_start(rope_r[:], consts[:, C_ROPER:C_ROPER + 1024]
                         .rearrange("p (a t f) -> p a t f", a=2, t=2)).then_inc(in_tables, 16)
            sp.dma_start(rope_a[:], consts[:, C_ROPEA:C_ROPEA + 512]
                         .rearrange("p (a t f) -> p a t f", a=2, t=2)).then_inc(in_tables, 16)
            sp.dma_start(gains[:, 0, :], q_norm[0:1, :].broadcast_to([P, AD])).then_inc(in_tables, 16)
            sp.dma_start(gains[:, 1, :], k_norm[0:1, :].broadcast_to([P, AD])).then_inc(in_tables, 16)
            sp.dma_start(dist[:], consts[:, C_DIST:C_DIST + 512]
                         .rearrange("p (t f) -> p t f", t=2)).then_inc(in_tables, 16)
            sp.dma_start(decin[:, 0:RH], decay_f[0:1, :].broadcast_to([P, RH])).then_inc(in_decay, 16)
            sp.dma_start(decin[:, RH:2 * RH], decay_b[0:1, :].broadcast_to([P, RH])).then_inc(in_decay, 16)
            x1_at = 2 * CHUNK_OF[("vr", 3)]
            mod2_at = 2 * CHUNK_OF[("ada", 5)]
            late_at = 2 * CHUNK_OF[("out", 0)]
            for n in range(6, NPRE):
                load(n)
                if n == x1_at:
                    full(sp, ("rT", "kr", 1, 3))
                    sp.dma_start(x1[:], x[0].rearrange("(t p) d -> p t d", p=P)).then_inc(in_x1, 16)
                if n == mod2_at:
                    full(sp, ("oT", RH - 1, 1))
                    sp.wait_ge(read["dve"], READ_AT[("ro", RH - 1, 1)])
                    sp.dma_start(mod2[4:5, :], b_ada[:, 2048:6144]).then_inc(in_mod2, 16)
                    sp.dma_start(b1_rows[:], b1[0]).then_inc(in_b1, 16)
                if n == late_at:
                    full(sp, ("ret_o", 1, 3))
                    sp.dma_start(norm2_b[:], norm2[0:1, :].broadcast_to([P, D])).then_inc(in_norm2, 16)
                    sp.dma_start(b2_sb[:], b2[0]).then_inc(in_late, 16)
                    sp.dma_start(wr_sb[:], w_router[0].rearrange("(k p) e -> p k e", p=P)).then_inc(in_late, 16)
                    sp.dma_start(ident2[:], consts[:, C_ID2:C_ID2 + CAP]).then_inc(in_late, 16)
                    sp.dma_start(slot_no[:], consts[:, C_SLOT:C_SLOT + P]).then_inc(in_late, 16)
                    sp.dma_start(tri[:], consts[:, C_TRI:C_TRI + P]).then_inc(in_late, 16)
                    sp.dma_start(br_b[:], b_router[0:1, :].broadcast_to([P, E])).then_inc(in_late, 16)

            def expert_half(m, src, r):
                s, _ = raw_count(m)
                if isinstance(r, int) and m < 12:
                    if s < 8:
                        sp.wait_ge(*chunk_released((NPRE - 8 + (s - NPRE) % 8) // 2))
                    elif s < 10:
                        sp.wait_ge(h2_split, 2)
                else:
                    sp.wait_ge(g_full, m // 2 - 5 + 6 * r)
                sp.dma_start(raw[s][:], src).then_inc(raw_in[s], 16)

            def w1_half(e, j):
                return w1[0, e, 512 * (j % 2):512 * (j % 2) + 512, CW * (j // 2):CW * (j // 2) + CW] \
                    .rearrange("(k p) n -> p k n", p=P)

            def w2_half(e, j):
                return w2[0, e, 512 * (j % 2):512 * (j % 2) + 512, CW * (j // 2):CW * (j // 2) + CW] \
                    .rearrange("(k p) n -> p k n", p=P)

            def round_(i, p, q0, r):
                if not is_at(i, E):
                    for j in range(8):
                        expert_half(2 * q0 + j, w1_half(i, j), r)
                if not is_at(i, 0):
                    for j in range(4):
                        expert_half(2 * q0 + (0 if is_at(i, E) else 8) + j, w2_half(i - 1, j), r)

            full(sp, ("bc", 7))
            all_rounds(sp, round_)
            with more_passes(sp) as p:
                all_rounds(sp, round_, p)
            sp.wait_ge(out_done, 2)
            sp.dma_start(out[0].rearrange("(t p) d -> p t d", p=P), x1[:]).then_inc(y_out, 16)
            sp.wait_ge(y_out, 16)

        @block.scalar
        def _(act):
            st = Steps(act, "act")

            def split_high(n):
                act.wait_ge(raw_in[n % 8], 16 * (n // 8 + 1))
                if n >= 4:
                    act.wait_ge(*chunk_released(n // 2 - 2))
                act.activation(wh[n % 4][:], raw[n % 8][:], ACT.Copy).then_inc(h_ready, 1)

            def done(ins):
                ins.then_inc(read["act"], 1)

            stds = [0]

            def std(col, n):
                stds[0] += 1
                act.wait_ge(var_ready, stds[0])
                act.activation(stat[:, col + n:col + 2 * n], stat[:, col:col + n], ACT.Sqrt).then_inc(std_ready, 1)

            split_high(0)
            split_high(1)
            act.wait_ge(in_decay, 32)
            st.link(act.activation(lowdec[:], decin[:], ACT.Abs))
            st.link(act.activation(lowdec[:], lowdec[:], ACT.Exp, scale=-1.0))
            act.activation(lowdec[:], lowdec[:], ACT.Ln, bias=1.0).then_inc(dec_abs, 1)
            act.wait_ge(in_cols, 16)
            act.activation(cc[:].rearrange("p k s -> p s k"), cols_in[:, 0:2, :], ACT.Sigmoid).then_inc(sigm, 1)
            act.wait_ge(in_rows, 32)
            for t in range(4):
                act.activation(xT[:, 2 * t:2 * t + 2, :].rearrange("p a b -> p (a b)"), rows[:, t, :], ACT.Square,
                               accum_out=stat[:, t:t + 1]).then_inc(squares, 1)
            std(0, 4)

            for n, (name, reader) in enumerate(PLAN):
                for chunk in FIRST_TILE.get(n, []):
                    if chunk + 1 < len(CHUNKS):
                        split_high(2 * chunk + 2)
                        split_high(2 * chunk + 3)
                kind = name[0]
                if name[:2] == ("proj", "vr") and name[3] == 0:
                    h = name[2]
                    act.wait_ge(exponent, h + 1)
                    act.activation(decay[:, 2:4, :], decay[:, 2:4, :], ACT.Exp).then_inc(exp_done, 1)
                    act.activation(decay[:, 0:2, :], dist[:], ACT.Exp, scale=logdec[:, h:h + 1],
                                   bias=lowdec[:, h:h + 1]).then_inc(exp_done, 1)
                    act.activation(decay2[:].rearrange("p (a b) -> p a b", b=SEQ), dist[:], ACT.Exp,
                                   scale=decin[:, RH + h:RH + h + 1],
                                   bias=lowdec[:, RH + h:RH + h + 1]).then_inc(exp_done, 1)
                if kind == "ada":
                    j = name[1]
                    dst = mod1[0:4, j * CW:(j + 1) * CW] if j < 4 else mod2[0:4, (j - 4) * CW:(j - 3) * CW]
                    full(act, name)
                    done(act.activation(dst, bank_of(name)[0:4, :], ACT.Copy))
                elif kind == "cols":
                    for k in range(KB):
                        act.wait_ge(h_full, k + 1)
                        act.activation(hH[:, k, :], xT[:, k, :], ACT.Copy).then_inc(h_rounded, 1)
                elif kind == "proj":
                    _, w, c_, t = name
                    if w in ("qa", "ka"):
                        r = ROPED.index(("rT", w, c_, t))
                        if r >= 2:
                            full(act, ROPED[r - 2])
                        full(act, name)
                        if w == "qa":
                            done(act.activation(roped[r % 2][:], bank_of(name)[:], ACT.Copy))
                            std(8, 4)
                        else:
                            st.link(act.activation(roped[r % 2][:, 0:256], bank_of(name)[:, 0:256], ACT.Copy))
                            done(act.activation(va[:, t, :], bank_of(name)[:, 256:512], ACT.Copy))
                            std(8, 2)
                    elif w == "vr":
                        full(act, name)
                        done(act.activation(v[:, t, :], bank_of(name)[:], ACT.Copy))
                    elif w == "gr":
                        full(act, name)
                        act.activation(g[:, t - 2, :], bank_of(name)[:], ACT.Sigmoid).then_inc(sg_ready, 1)
                    elif w in ("gate_r", "gate_a"):
                        dst = gate_r if w == "gate_r" else gate_a
                        full(act, name)
                        done(act.activation(dst[:, t - 2, c_ * CW:(c_ + 1) * CW], bank_of(name)[:], ACT.Sigmoid))
                elif kind == "rT":
                    _, w, c_, t = name
                    full(act, name)
                    src = bank_of(name)[:].rearrange("p (a b) -> p a b", b=P)
                    if w == "qa":
                        dst = qaT[:, 4 * c_:4 * c_ + 4, (t - 2) * P:(t - 1) * P]
                    elif w == "ka":
                        dst, src = kaT[:, :, t * P:(t + 1) * P], src[:, 0:2, :]
                    elif w == "qr":
                        dst = qrT[:, :, (t - 2) * P:(t - 1) * P]
                    else:
                        dst = krT[:, :, t * P:(t + 1) * P]
                    done(act.activation(dst, src, ACT.Copy))
                elif kind == "score":
                    _, h, t = name
                    u = 2 * h + t
                    full(act, name)
                    act.wait_ge(neg_max, u + 1)
                    if u >= 2:
                        full(act, ("pT", (u - 2) // 2, (u - 2) % 2))
                    done(act.activation(prob[u % 2][:], bank_of(name)[:], ACT.Exp, scale=AD ** -0.5,
                                        bias=stat[:, 24 + u % 2:25 + u % 2], accum_out=stat[:, 26 + u % 2:27 + u % 2]))
                elif kind == "pT":
                    _, h, t = name
                    full(act, name)
                    if h:
                        full(act, ("av", h - 1))
                    done(act.activation(probT[:, :, t * P:(t + 1) * P],
                                        bank_of(name)[:].rearrange("p (a b) -> p a b", b=P), ACT.Copy))
                elif kind == "ro":
                    _, h, t = name
                    full(act, name)
                    act.wait_ge(decay_ready, h + 1)
                    act.wait_ge(squares, 4 + 2 * h + t)
                    act.activation(decay2[:], bank_of(name)[:], ACT.Square,
                                   accum_out=stat[:, 16 + t:17 + t]).then_inc(squares, 1)
                    if t == 1:
                        std(16, 2)
                elif kind == "oT":
                    _, h, b = name
                    full(act, name)
                    done(act.activation(oT[:, 4 * h + 2 * b:4 * h + 2 * b + 2, :],
                                        bank_of(name)[:].rearrange("p (a b) -> p a b", b=SEQ), ACT.Copy))
                elif kind == "b1":
                    full(act, name)
                    done(act.activation(b1_cols[:], bank_of(name)[:].rearrange("p (a b) -> p a b", b=E), ACT.Copy))
                elif kind == "yT":
                    full(act, name)
                    j = name[1]
                    act.activation(yH[:, 2 * j:2 * j + 2, :], bank_of(name)[:].rearrange("p (a b) -> p a b", b=SEQ),
                                   ACT.Copy).then_inc(yH_ready, 1)
                elif kind == "bc":
                    full(act, name)
                    j = name[1]
                    done(act.activation(bc[:, j // 2, (j % 2) * CW:(j % 2 + 1) * CW], bank_of(name)[:], ACT.Copy))
                elif kind == "h2T":
                    full(act, name)
                    j = name[1]
                    done(act.activation(h2T[:, 2 * j:2 * j + 2, :], bank_of(name)[:].rearrange("p (a b) -> p a b", b=SEQ),
                                        ACT.Copy))
                if name == ("ada", 4):
                    for j in range(4):
                        act.activation(oH[:, 4 * j:4 * j + 4, :], oT[:, 4 * j:4 * j + 4, :], ACT.Copy).then_inc(oH_ready, 1)
                if name == ("b1", 0):
                    act.wait_ge(oL_ready, 4)
                    for j in range(2):
                        act.activation(aH[:, 4 * j:4 * j + 4, :], oaT[:, 4 * j:4 * j + 4, :], ACT.Copy).then_inc(oH_ready, 1)
                if name == ("bc", 7):
                    for t in range(2):
                        act.wait_ge(x1_ready, t + 1)
                        act.wait_ge(squares, 4 + 2 * RH + t)
                        act.activation(junk2[:], x1[:, t, :], ACT.Square, accum_out=stat[:, t:t + 1]).then_inc(squares, 1)
                    std(0, 2)
                    for t in range(2):
                        act.wait_ge(h2_ready, t + 1)
                        act.activation(h2H[:, t, :], h2[:, t, :], ACT.Copy).then_inc(h2_rounded, 1)
                if name == ("logits",):
                    for t in range(2):
                        act.wait_ge(neg_top, t + 1)
                        act.activation(comb[:, t, :], lp[:, t, 0:E], ACT.Exp, bias=route[:, t:t + 1]).then_inc(expl, 1)

            def expert_split(q, p, r):
                for m in (2 * q, 2 * q + 1):
                    s, count = raw_count(m)
                    act.wait_ge(raw_in[s], count + 16 * r)
                    if is_at(p, FIRST_PASS) and q < 2:
                        act.wait_ge(*chunk_released(len(CHUNKS) - 2 + q))
                    else:
                        act.wait_ge(g_full if m % 2 else first_half_used, q - 1 + 6 * r)
                    n = NPRE + m
                    act.activation(wh[n % 4][:], raw[s][:], ACT.Copy).then_inc(h_ready, 1)

            def gather_read(e):
                act.wait_ge(x_full, e + 1)
                for k in range(2):
                    act.activation(xg[:, 4 * k:4 * k + 4, :], banks[6 + k][:].rearrange("p (a b) -> p a b", b=P),
                                   ACT.Copy).then_inc(xg_ready, 1)

            def round_act(i, p, q0, r):
                e = i + E * p
                first, last = is_at(i, 0), is_at(i, E)
                if first:
                    expert_split(0, p, r)
                    gather_read(e)
                jobs = (4, 5) if last else (0, 1, 2, 3) if first else range(6)
                for n, j in enumerate(jobs):
                    q = q0 + n
                    if not (last and j == 5):
                        expert_split(q + 1, p, r)
                    if n == 4 and not is_at(i, E - 1):
                        gather_read(e + 1)
                    if j < 4:
                        act.wait_ge(g_full, q + 1 + 6 * r)
                        if j == 0 and not (first and is_at(p, FIRST_PASS)):
                            act.wait_ge(t_full, e)
                        act.activation(a_sb[:, j * CW:(j + 1) * CW], banks[4 + q % 2][:], ACT.Copy).then_inc(a_read, 1)
                    if n == 0 and not first:
                        act.wait_ge(clipped, e)
                        act.activation(sig[:], gate[:], ACT.Sigmoid, scale=ALPHA).then_inc(sig_ready, 1)
                    if n == (0 if last else 1) and not first:
                        act.wait_ge(act_ready, e)
                        if not (is_at(i, 1) and is_at(p, FIRST_PASS)):
                            act.wait_ge(o_read, 2 * (e - 1))
                        act.activation(act_hl[:, :, 0:CAP], gate[:].rearrange("p (k c) -> p k c", c=CAP),
                                       ACT.Copy).then_inc(act_high, 1)
                if first:
                    gather_read(e + 1)

            all_rounds(act, round_act)
            with more_passes(act) as p:
                all_rounds(act, round_act, p)

        @block.vector
        def _(dve):
            st = Steps(dve, "dve")

            def split_low(n):
                dve.wait_ge(h_ready, n + 1)
                dve.tensor_tensor(wl[n % 8][:], raw[n % 8][:], wh[n % 4][:].bitcast(f32), ALU.subtract) \
                    .then_inc(l_ready, 1)

            def done(ins):
                ins.then_inc(read["dve"], 1)

            calls = [0]

            def rsqrt(col, n, count):
                calls[0] += 1
                var, r, t = stat[:, col:col + n], stat[:, col + n:col + 2 * n], stat[:, 28:28 + n]
                dve.tensor_scalar(var, var, 1.0 / count, EPS, ALU.mult, ALU.add).then_inc(var_ready, 1)
                dve.wait_ge(std_ready, calls[0])
                st.link(dve.reciprocal(r, r))
                st.link(dve.tensor_tensor(t, r, r, ALU.mult))
                st.link(dve.tensor_tensor(t, t, var, ALU.mult))
                st.link(dve.tensor_scalar(t, t, -0.5, 1.5, ALU.mult, ALU.add))
                st.link(dve.tensor_tensor(r, r, t, ALU.mult))

            split_low(0)
            split_low(1)
            dve.wait_ge(in_decay, 32)
            dve.wait_ge(dec_abs, 1)
            st.link(dve.tensor_scalar(logdec[:], decin[:], 0.0, None, ALU.max))
            st.link(dve.tensor_tensor(logdec[:], logdec[:], lowdec[:], ALU.add))
            st.link(dve.tensor_scalar(logdec[:], logdec[:], -1.0, None, ALU.mult))
            st.link(dve.tensor_scalar(lowdec[:], logdec[:], float(CTX), None, ALU.mult))
            dve.tensor_scalar(decin[:], logdec[:], -1.0, None, ALU.mult).then_inc(dec_ready, 1)
            st.link(dve.memset(silu_c[:].bitcast(f32), 0.0))
            dve.wait_ge(sigm, 1)
            st.link(dve.tensor_tensor(cc[:].rearrange("p k s -> p s k"), cc[:].rearrange("p k s -> p s k"),
                                      cols_in[:, 0:2, :], ALU.mult))
            st.link(dve.tensor_copy(silu_c[:, :, 0:2], cc[:]))
            dve.tensor_tensor(silu_c[:, :, 2:4], cc[:], silu_c[:, :, 0:2].bitcast(f32), ALU.subtract) \
                .then_inc(silu_ready, 1)
            dve.wait_ge(squares, 4)
            rsqrt(0, 4, D)
            for t in range(4):
                dve.tensor_scalar(rows[:, t, :], rows[:, t, :], stat[:, 4 + t:5 + t], None, ALU.mult).then_inc(normed, 1)

            def rope(r, src, table, heads, width, t):
                dst = roped[r % 2]
                n = heads * width
                q = width // 4
                sv = src.rearrange("p (h a s f) -> p h a s f", a=2, s=2, f=q)
                dv = ropes[:, 0:n].rearrange("p (h a s f) -> p h a s f", a=2, s=2, f=q)
                tv = table[:, 1, t - 2, :].rearrange("p (a s f) -> p a s f", s=2, f=q)
                for s_ in range(2):
                    for h in range(heads):
                        ins = dve.tensor_tensor(dv[:, h, :, s_, :], sv[:, h, :, 1 - s_, :], tv[:, :, s_, :], ALU.mult)
                st.link(ins)
                sw = src.rearrange("p (h w) -> p h w", w=width)
                dw = dst[:, 0:n].rearrange("p (h w) -> p h w", w=width)
                cos = table[:, 0, t - 2, :].unsqueeze(1).broadcast_to([P, heads, width])
                last = dve.tensor_tensor(dw, sw, cos, ALU.mult)
                return last, n

            for n, (name, reader) in enumerate(PLAN):
                for chunk in FIRST_TILE.get(n, []):
                    if chunk + 1 < len(CHUNKS):
                        split_low(2 * chunk + 2)
                        split_low(2 * chunk + 3)
                kind = name[0]
                if kind == "xT":
                    full(dve, name)
                    done(dve.tensor_copy(xT[:, name[1], :], bank_of(name)[:]))
                elif kind == "cols":
                    full(dve, name)
                    was_read(dve, ("xT", KB - 1))
                    m = bank_of(name)[:, 0:32].rearrange("p (a k s) -> p a k s", a=2, s=2)
                    st.link(dve.tensor_scalar(scale1[:], m[:, 1], 1.0, None, ALU.add))
                    st.link(dve.tensor_tensor(scale1[:], scale1[:],
                                              cols_in[:, 2, :].unsqueeze(2).broadcast_to([P, KB, 2]), ALU.mult))
                    ins = dve.tensor_copy(shift1[:], m[:, 0])
                    done(ins)
                    was_read(dve, name)
                    for k in range(KB):
                        for s_, cols in ((1, slice(0, CTX)), (0, slice(CTX, CTX + SEQ))):
                            ins = dve.tensor_scalar(xT[:, k, cols], xT[:, k, cols], scale1[:, k, s_:s_ + 1],
                                                    shift1[:, k, s_:s_ + 1], ALU.mult, ALU.add)
                            if s_:
                                st.link(ins)
                        ins.then_inc(h_full, 1)
                    dve.wait_ge(h_full, KB)
                    for k in range(KB):
                        dve.wait_ge(h_rounded, k + 1)
                        dve.tensor_tensor(hL[:, k, :], xT[:, k, :], hH[:, k, :].bitcast(f32), ALU.subtract) \
                            .then_inc(h_split, 1)
                elif kind == "proj":
                    _, w, c_, t = name
                    if w in ("qa", "ka"):
                        was_read(dve, name)
                        r = ROPED.index(("rT", w, c_, t))
                        if r:
                            in_roped(dve, r - 1)
                        heads = 4 if w == "qa" else 2
                        nn = heads * AD
                        q = roped[r % 2]
                        qv = q[:, 0:nn].rearrange("p (h w) -> p h w", w=AD)
                        if r == 0:
                            dve.wait_ge(in_tables, 80)
                        st.link(dve.tensor_tensor(ropes[:, 0:nn], q[:, 0:nn], q[:, 0:nn], ALU.mult))
                        st.link(dve.tensor_reduce(stat[:, 8:8 + heads], ropes[:, 0:nn].rearrange("p (h w) -> p h w", w=AD),
                                                  AX.X, ALU.add))
                        rsqrt(8, heads, AD)
                        st.link(dve.tensor_tensor(qv, qv, stat[:, 8 + heads:8 + 2 * heads].unsqueeze(2)
                                                  .broadcast_to([P, heads, AD]), ALU.mult))
                        ins = dve.tensor_tensor(qv, qv, gains[:, int(w == "ka"):int(w == "ka") + 1, :]
                                                .broadcast_to([P, heads, AD]), ALU.mult)
                        if t >= 2:
                            st.link(ins)
                            last, nn = rope(r, q[:, 0:nn], rope_a, heads, AD, t)
                            st.link(last)
                            ins = dve.tensor_tensor(q[:, 0:nn], q[:, 0:nn], ropes[:, 0:nn], ALU.add)
                        ins.then_inc(roped_ready, 1)
                    elif w in ("qr", "kr"):
                        r = ROPED.index(("rT", w, c_, t))
                        in_roped(dve, r - 1)
                        full(dve, ROPED[r - 2])
                        full(dve, name)
                        if t < 2:
                            done(dve.tensor_copy(roped[r % 2][:], bank_of(name)[:]))
                        else:
                            last, nn = rope(r, bank_of(name)[:], rope_r, 2, RQK, t)
                            done(last)
                            was_read(dve, name)
                            dve.tensor_tensor(roped[r % 2][:], roped[r % 2][:], ropes[:], ALU.add).then_inc(roped_ready, 1)
                    elif w == "gr":
                        full(dve, name)
                        dve.wait_ge(sg_ready, 2 * c_ + t - 1)
                        done(dve.tensor_tensor(g[:, t - 2, :], bank_of(name)[:], g[:, t - 2, :], ALU.mult))
                elif kind == "score":
                    _, h, t = name
                    u = 2 * h + t
                    if u:
                        dve.wait_ge(neg_max, u)
                    if u >= 2:
                        was_read(dve, ("score", (u - 2) // 2, (u - 2) % 2))
                    full(dve, name)
                    st.link(dve.tensor_reduce(stat[:, 22:23], bank_of(name)[:], AX.X, ALU.max))
                    dve.tensor_scalar(stat[:, 24 + u % 2:25 + u % 2], stat[:, 22:23], -AD ** -0.5, None, ALU.mult) \
                        .then_inc(neg_max, 1)
                elif kind == "pT":
                    pass
                elif kind == "av":
                    h = name[1]
                    full(dve, name)
                    done(dve.tensor_copy(oaT[:, h, :], bank_of(name)[:, 0:SEQ]))
                elif kind == "rs":
                    _, h, b = name
                    full(dve, name)
                    dve.wait_ge(decay_ready, h + 1)
                    done(dve.scalar_tensor_tensor(decay[:, 2 * b:2 * b + 2, :].rearrange("p a b -> p (a b)"),
                                                  bank_of(name)[:], RQK ** -0.5,
                                                  decay[:, 2 * b:2 * b + 2, :].rearrange("p a b -> p (a b)"),
                                                  ALU.mult, ALU.mult))
                elif kind == "ro" and name[2] == 1:
                    h = name[1]
                    dve.wait_ge(squares, 4 + 2 * h + 2)
                    rsqrt(16, 2, RV)
                    for t in range(2):
                        full(dve, ("ro", h, t))
                        done(dve.scalar_tensor_tensor(g[:, t, :], bank_of(("ro", h, t))[:], stat[:, 18 + t:19 + t],
                                                      g[:, t, :], ALU.mult, ALU.mult))
                elif kind == "ret_o":
                    _, col, t = name
                    full(dve, name)
                    dst = gate_r[:, t - 2, col * CW:(col + 1) * CW]
                    done(dve.tensor_tensor(dst, bank_of(name)[:], dst, ALU.mult))
                elif kind == "attn_o":
                    _, col, t = name
                    full(dve, name)
                    a = gate_a[:, t - 2, col * CW:(col + 1) * CW]
                    y_ = gate_r[:, t - 2, col * CW:(col + 1) * CW]
                    done(dve.tensor_tensor(a, bank_of(name)[:], a, ALU.mult))
                    was_read(dve, name)
                    dve.tensor_tensor(y_, y_, a, ALU.add).then_inc(y_ready, 1)
                elif kind == "yT":
                    j = name[1]
                    dve.wait_ge(yH_ready, j + 1)
                    done(dve.tensor_tensor(yL[:, 2 * j:2 * j + 2, :], bank_of(name)[:].rearrange("p (a b) -> p a b", b=SEQ),
                                           yH[:, 2 * j:2 * j + 2, :].bitcast(f32), ALU.subtract))
                elif kind == "out":
                    _, col, t = name
                    cols = slice(col * CW, (col + 1) * CW)
                    if (col, t) == (0, 2):
                        was_read(dve, ("bc", 1))
                        dve.wait_ge(in_x1, 16)
                    full(dve, name)
                    done(dve.tensor_tensor(h2[:, t - 2, cols], bank_of(name)[:], bc[:, 0, cols], ALU.mult))
                    was_read(dve, name)
                    ins = dve.tensor_tensor(x1[:, t - 2, cols], x1[:, t - 2, cols], h2[:, t - 2, cols], ALU.add)
                    if col == 1:
                        ins.then_inc(x1_ready, 1)
                    else:
                        st.link(ins)
                elif kind == "logits":
                    full(dve, name)
                    dve.wait_ge(in_late, 96)
                    st.link(dve.memset(lp[:], -3.0e38))
                    st.link(dve.memset(rep[:], -3.0e38))
                    lg = bank_of(name)[:, 0:2 * E].rearrange("p (t e) -> p t e", e=E)
                    done(dve.tensor_tensor(lp[:, :, 0:E], lg, br_b[:].unsqueeze(1).broadcast_to([P, 2, E]), ALU.add))
                    was_read(dve, name)
                    for t in range(2):
                        ins = dve.max(out=top[:, t, :], in_=lp[:, t, :])
                        st.link(ins)
                        dve.tensor_scalar(route[:, t:t + 1], top[:, t, 0:1], -1.0, None, ALU.mult).then_inc(neg_top, 1)
                        st.link(dve.tensor_copy(rep[:, t, 0:TOPK], top[:, t, 0:TOPK]))
                        st.link(dve.match_replace(out=lm[:, t, :], in_to_replace=rep[:, t, :], in_values=lp[:, t, :],
                                                  imm_value=-3.2e38))
                    dve.tensor_tensor(chosen[:], lm[:, :, 0:E], lp[:, :, 0:E], ALU.not_equal).then_inc(chosen_ready, 1)
                    dve.wait_ge(chosen_ready, 1)
                    dve.wait_ge(expl, 2)
                    st.link(dve.tensor_tensor(comb[:], comb[:], chosen[:], ALU.mult))
                    st.link(dve.tensor_reduce(route[:, 2:4], comb[:], AX.X, ALU.add))
                    st.link(dve.reciprocal(route[:, 2:4], route[:, 2:4]))
                    dve.tensor_tensor(comb[:], comb[:], route[:, 2:4].unsqueeze(2).broadcast_to([P, 2, E]), ALU.mult) \
                        .then_inc(comb_ready, 1)
                elif kind == "rank":
                    full(dve, name)
                    st.link(dve.tensor_reduce(most[:], bank_of(name)[:, 2 * E:3 * E], AX.X, ALU.max))
                    dve.tensor_copy(most_int[:], most[:]).then_inc(most_ready, 1)
                    dve.wait_ge(comb_ready, 1)
                    rk = bank_of(name)[:, 0:2 * E].rearrange("p (t e) -> p t e", e=E)
                    done(dve.scalar_tensor_tensor(rank[:], rk, 1.0, chosen[:], ALU.add, ALU.mult))
                    was_read(dve, name)
                    dve.tensor_scalar(rank[:], rank[:], -1.0, None, ALU.add).then_inc(rank_ready, 1)
                elif kind == "combT":
                    full(dve, name)
                    done(dve.tensor_copy(combT[:], bank_of(name)[0:E, 0:SEQ]))
                if n + 1 < len(PLAN) and PLAN[n + 1][0][0] == "pT":
                    _, h, t = PLAN[n + 1][0]
                    u = 2 * h + t
                    was_read(dve, ("score", h, t))
                    if u:
                        dve.wait_ge(prob_ready, u)
                    st.link(dve.reciprocal(stat[:, 21:22], stat[:, 26 + u % 2:27 + u % 2]))
                    dve.tensor_scalar(prob[u % 2][:], prob[u % 2][:], stat[:, 21:22], None, ALU.mult).then_inc(prob_ready, 1)
                if name == ("ada", 4):
                    for j in range(4):
                        dve.wait_ge(oH_ready, j + 1)
                        dve.tensor_tensor(oL[:, 4 * j:4 * j + 4, :], oT[:, 4 * j:4 * j + 4, :],
                                          oH[:, 4 * j:4 * j + 4, :].bitcast(f32), ALU.subtract).then_inc(oL_ready, 1)
                if name == ("b1", 0):
                    for j in range(2):
                        dve.wait_ge(oH_ready, 5 + j)
                        dve.tensor_tensor(aL[:, 4 * j:4 * j + 4, :], oaT[:, 4 * j:4 * j + 4, :],
                                          aH[:, 4 * j:4 * j + 4, :].bitcast(f32), ALU.subtract).then_inc(oL_ready, 1)
                if name == ("bc", 7):
                    dve.wait_ge(in_norm2, 16)
                    was_read(dve, ("bc", 7))
                    st.link(dve.scalar_tensor_tensor(bc[:, 2, :], bc[:, 2, :], 1.0, norm2_b[:], ALU.add, ALU.mult))
                    dve.wait_ge(squares, 4 + 2 * RH + 2)
                    rsqrt(0, 2, D)
                    for t in range(2):
                        st.link(dve.scalar_tensor_tensor(h2[:, t, :], x1[:, t, :], stat[:, 2 + t:3 + t], bc[:, 2, :],
                                                         ALU.mult, ALU.mult))
                        dve.tensor_tensor(h2[:, t, :], h2[:, t, :], bc[:, 1, :], ALU.add).then_inc(h2_ready, 1)
                    for t in range(2):
                        dve.wait_ge(h2_rounded, t + 1)
                        dve.tensor_tensor(h2L[:, t, :], h2[:, t, :], h2H[:, t, :].bitcast(f32), ALU.subtract) \
                            .then_inc(h2_split, 1)

            def expert_split(q, r):
                for m in (2 * q, 2 * q + 1):
                    s, _ = raw_count(m)
                    n = NPRE + m
                    dve.wait_ge(h_ready, n + 1 + 12 * r)
                    dve.tensor_tensor(wl[s][:], raw[s][:], wh[n % 4][:].bitcast(f32), ALU.subtract).then_inc(l_ready, 1)

            def bias_of(i, block):
                return b1_cols[:, 8 * block:8 * block + 8, bass.ds(i, 1)].broadcast_to([P, 8, CAP])

            def turned_read(i, p):
                e = i + E * p
                dve.wait_ge(t_full, e + 1)
                if not (is_at(i, 0) and is_at(p, FIRST_PASS)):
                    dve.wait_ge(act_low, e)
                for part, (dst, bank) in enumerate(((gate, banks[6]), (up, banks[7]))):
                    dve.tensor_tensor(dst[:].rearrange("p (k c) -> p k c", c=CAP),
                                      bank[:].rearrange("p (k c) -> p k c", c=CAP), bias_of(i, part), ALU.add) \
                        .then_inc(t_read, 1)

            def round_dve(i, p, q0, r):
                e = i + E * p
                first, last = is_at(i, 0), is_at(i, E)
                used = not (is_at(i, 1) and is_at(p, FIRST_PASS))
                if first:
                    expert_split(0, r)
                jobs = (4, 5) if last else (0, 1, 2, 3) if first else range(6)
                for n, j in enumerate(jobs):
                    q = q0 + n
                    if not (last and j == 5):
                        expert_split(q + 1, r)
                    if n == (1 if last else 2) and not first:
                        dve.wait_ge(tp_full, e)
                        if used:
                            dve.wait_ge(scattered, e - 1)
                        dve.tensor_copy(spreadT[:], banks[6][:, 0:SEQ]).then_inc(tp_read, 1)
                    if n == 5:
                        turned_read(i, p)
                    if j >= 4:
                        dve.wait_ge(g_full, q + 1 + 6 * r)
                        if j == 4 and used:
                            dve.wait_ge(scattered, e - 1)
                        dve.tensor_copy(out2[:, (j - 4) * CW:(j - 3) * CW], banks[4 + q % 2][:]).then_inc(o_read, 1)
                if first:
                    turned_read(i, p)

            all_rounds(dve, round_dve)
            dve.wait_ge(scattered, E)
            with more_passes(dve) as p:
                all_rounds(dve, round_dve, p)
                dve.wait_ge(scattered, E * p + E)
            for t in range(2):
                for col in range(2):
                    cols = slice(col * CW, (col + 1) * CW)
                    part = a_sb[:, (2 * t + col) * CW:(2 * t + col + 1) * CW]
                    st.link(dve.tensor_tensor(part, banks[2 * t + col][:], bc[:, 3, cols], ALU.mult))
                    ins = dve.tensor_tensor(x1[:, t, cols], x1[:, t, cols], part, ALU.add)
                    if col:
                        ins.then_inc(out_done, 1)
                    else:
                        st.link(ins)

        @block.gpsimd
        def _(pool):
            st = Steps(pool, "pool")
            pool.wait_ge(dec_ready, 1)
            for h in range(RH):
                if h:
                    was_read(pool, ("ro", h - 1, 1))
                else:
                    pool.wait_ge(roped_ready, 8)
                    pool.wait_ge(in_tables, 80)
                d2 = decay2[:].rearrange("p (a b) -> p a b", b=SEQ)
                st.link(pool.tensor_scalar(decay[:, 2:4, :], dist[:], 0.0, None, ALU.max))
                st.link(pool.tensor_scalar(decay[:, 2:4, :], decay[:, 2:4, :], logdec[:, h:h + 1], None, ALU.mult))
                st.link(pool.tensor_scalar(d2, dist[:], 0.0, None, ALU.min))
                st.link(pool.tensor_scalar(d2, d2, decin[:, RH + h:RH + h + 1], None, ALU.mult))
                pool.tensor_tensor(decay[:, 2:4, :], decay[:, 2:4, :], d2, ALU.add).then_inc(exponent, 1)
                pool.wait_ge(exp_done, 3 * h + 3)
                pool.tensor_tensor(decay[:, 0:2, :], decay[:, 0:2, :], d2, ALU.add).then_inc(decay_ready, 1)

            full(pool, ("ret_o", 1, 3))
            pool.memset(ones[:], 1.0).then_inc(chain["pool"], 1)
            st.n += 1
            pool.wait_ge(rank_ready, 1)
            pool.wait_ge(in_late, 96)

            def pool_waits(semaphore, value):
                pool.wait_ge(semaphore, value)
                if not isinstance(value, int):
                    pool.nop(nofuse=True)

            def build_onehot(i, e):
                if not is_at(e, 0):
                    pool_waits(onehot_ready, 2 * e)
                pool.tensor_copy(now_rank[:], rank[:, :, bass.ds(i, 1)]).then_inc(columns_ready, 1)
                pool_waits(columns_ready, 3 * e + 1 if is_at(i, 0) else 3 * e - 1)
                for t in range(2):
                    pool.tensor_scalar(onehot[:, t, :], slot_no[:, 0:CAP], now_rank[:, t, :], None,
                                       ALU.is_equal).then_inc(onehot_ready, 1)

            def build_spread(i, e):
                if not is_at(e, 0):
                    pool_waits(spread_ready, 2 * e)
                pool.tensor_copy(own_rank[:], rank[:, :, bass.ds(i, 1)]).then_inc(columns_ready, 1)
                pool.tensor_copy(own_comb[:], comb[:, :, bass.ds(i, 1)]).then_inc(columns_ready, 1)
                pool_waits(columns_ready, 3 * e + 3 if is_at(i, E - 1) else 3 * e + 4)
                for t in range(2):
                    pool.tensor_scalar(spread[:, t, :], slot_no[:], own_rank[:, t, :],
                                       own_comb[:, t, :], ALU.is_equal, ALU.mult).then_inc(spread_ready, 1)

            def round_pool(i, p, q0, r):
                e = i + E * p
                first = is_at(i, 0)
                if is_at(i, E):
                    return
                if first:
                    if not is_at(p, FIRST_PASS):
                        pool_waits(spread_ready, 2 * e)
                        pool_waits(onehot_ready, 2 * e)
                        pool.tensor_scalar(rank[:], rank[:], -float(CAP), None, ALU.add).then_inc(shifted, 1)
                        pool_waits(shifted, p)
                    build_onehot(i, e)
                if not is_at(i, E - 1):
                    pool_waits(x_full, e + 1)
                    build_onehot(i + 1, e + 1)
                if not (first and is_at(p, FIRST_PASS)):
                    pool_waits(tp_full, e)
                build_spread(i, e)
                pool_waits(t_read, 2 * e + 2)
                pool.tensor_scalar(gate[:], gate[:], LIMIT, None, ALU.min).then_inc(clipped, 1)
                pool.tensor_scalar(up[:], up[:], LIMIT, -LIMIT, ALU.min, ALU.max).then_inc(up_steps, 1)
                pool_waits(up_steps, 3 * e + 1)
                pool.tensor_scalar(up[:], up[:], 1.0, None, ALU.add).then_inc(up_steps, 1)
                pool_waits(clipped, e + 1)
                pool_waits(up_steps, 3 * e + 2)
                pool.tensor_tensor(up[:], up[:], gate[:], ALU.mult).then_inc(up_steps, 1)
                pool_waits(up_steps, 3 * e + 3)
                pool_waits(sig_ready, e + 1)
                pool.tensor_tensor(gate[:], up[:], sig[:], ALU.mult).then_inc(act_ready, 1)
                pool_waits(act_high, e + 1)
                pool.tensor_tensor(act_hl[:, :, CAP:2 * CAP], gate[:].rearrange("p (k c) -> p k c", c=CAP),
                                   act_hl[:, :, 0:CAP].bitcast(f32), ALU.subtract).then_inc(act_low, 1)

            all_rounds(pool, round_pool)
            with more_passes(pool) as p:
                all_rounds(pool, round_pool, p)

        @block.tensor
        def _(pe):
            def tile(name, emit, signal=True):
                n = TILE_AT[name]
                if n >= 8:
                    was_read(pe, PLAN[n - 8][0])
                last = emit(banks[n % 8])
                if signal:
                    last.then_inc(psum_full, 1)
                return last

            def halves(n):
                pe.wait_ge(l_ready, n + 1)

            def three(ps, hi, lo, n, k, start, stop):
                wslot, lslot, kk = (2 * n + k // 4) % 4, (2 * n + k // 4) % 8, k % 4
                pe.matmul(ps[:], hi, wh[wslot][:, kk, :], start=start, stop=False)
                pe.matmul(ps[:], hi, wl[lslot][:, kk, :], start=False, stop=False)
                return pe.matmul(ps[:], lo, wh[wslot][:, kk, :], start=False, stop=stop)

            def product(ps, hi, lo, n, cols, k0=0, start=True, stop=True):
                for k in range(KB):
                    if k % 4 == 0:
                        halves(2 * n + k // 4)
                    last = three(ps, hi[:, k0 + k, cols], lo[:, k0 + k, cols], n, k, start and k == 0, stop and k == KB - 1)
                return last

            def turn(ps, parts):
                for j, src in enumerate(parts):
                    last = pe.transpose(ps[0:src.shape[1], j * src.shape[0]:(j + 1) * src.shape[0]], src,
                                        ident[0:src.shape[0], 0:src.shape[0]])
                return last

            pe.wait_ge(in_ident, 32)
            pairs = {}
            for n, (name, reader) in enumerate(PLAN):
                kind = name[0]
                if kind == "xT":
                    k = name[1]
                    if k == 0:
                        pe.wait_ge(normed, 4)
                    tile(name, lambda ps: turn(ps, [rows[:, t, k * P:(k + 1) * P] for t in range(4)]))
                elif kind == "ada":
                    ch = CHUNK_OF[name]
                    if name[1] == 0:
                        pe.wait_ge(silu_ready, 1)

                    def emit(ps):
                        for k in range(KB):
                            if k % 4 == 0:
                                halves(2 * ch + k // 4)
                            ws, ls = (2 * ch + k // 4) % 4, (2 * ch + k // 4) % 8
                            pe.matmul(ps[:], silu_c[:, k, :], wh[ws][:, k % 4, :], start=k == 0, stop=False)
                            last = pe.matmul(ps[:], silu_c[:, k, :], wl[ls][:, k % 4, :], start=False, stop=k == KB - 1)
                        return last
                    tile(name, emit)
                elif kind == "cols":
                    was_read(pe, ("ada", 3))
                    pe.wait_ge(in_bada, 16)

                    def emit(ps):
                        for b in range(16):
                            last = pe.matmul(ps[:, 2 * b:2 * b + 2], mod1[:, b * P:(b + 1) * P], sel[:, 0:2],
                                             start=True, stop=True)
                        return last
                    tile(name, emit)
                elif kind == "proj":
                    _, w, c_, t = name
                    if name == ("proj", "qa", 0, 2):
                        pe.wait_ge(h_split, KB)
                    tile(name, lambda ps: product(ps, hH, hL, CHUNK_OF[(w, c_)], slice(t * P, (t + 1) * P)))
                elif kind == "rT":
                    r = ROPED.index(name)
                    in_roped(pe, r)
                    blocks = 2 if name[1] == "ka" else 4
                    tile(name, lambda ps: turn(ps, [roped[r % 2][:, b * P:(b + 1) * P] for b in range(blocks)]))
                elif kind == "score":
                    _, h, t = name
                    if h == 0:
                        was_read(pe, ("rT", "ka", 0, 3))
                    tile(name, lambda ps: pe.matmul(ps[:], qaT[:, h, t * P:(t + 1) * P], kaT[:, h // (AH // AKV), :],
                                                    start=True, stop=True))
                elif kind == "pT":
                    _, h, t = name
                    pe.wait_ge(prob_ready, 2 * h + t + 1)
                    tile(name, lambda ps: turn(ps, [prob[t][:, b * P:(b + 1) * P] for b in range(4)]))
                elif kind == "av":
                    h = name[1]
                    kv = h // (AH // AKV)
                    was_read(pe, ("pT", h, 1))

                    def emit(ps):
                        for b in range(4):
                            last = pe.matmul(ps[:, 0:SEQ], va[:, b, kv * AD:(kv + 1) * AD], probT[:, b, :],
                                             start=b == 0, stop=b == 3)
                        return last
                    tile(name, emit)
                elif kind == "rs":
                    _, h, b = name
                    hh = h % 2
                    was_read(pe, ("rT", "kr", h // 2, 3))

                    def emit(ps):
                        for m in range(2):
                            for k in range(2):
                                last = pe.matmul(ps[:, m * SEQ:(m + 1) * SEQ],
                                                 krT[:, 2 * hh + k, (2 * b + m) * P:(2 * b + m + 1) * P],
                                                 qrT[:, 2 * hh + k, :], start=k == 0, stop=k == 1)
                        return last
                    tile(name, emit)
                elif kind == "ro":
                    _, h, t = name
                    was_read(pe, ("rs", h, 1))
                    was_read(pe, ("proj", "vr", h, 3))

                    def emit(ps):
                        for m in range(4):
                            last = pe.matmul(ps[:], decay[:, m, t * P:(t + 1) * P], v[:, m, :], start=m == 0, stop=m == 3)
                        return last
                    tile(name, emit)
                elif kind == "oT":
                    _, h, b = name
                    was_read(pe, ("ro", h, 1))
                    tile(name, lambda ps: turn(ps, [g[:, t, (2 * b + j) * P:(2 * b + j + 1) * P]
                                                    for j in range(2) for t in range(2)]))
                elif kind == "b1":
                    pe.wait_ge(in_b1, 16)
                    tile(name, lambda ps: turn(ps, [b1_rows[:, b * P:(b + 1) * P] for b in range(16)]))
                elif kind == "ret_o":
                    _, col, t = name
                    if name == ("ret_o", 0, 2):
                        pe.wait_ge(oL_ready, 4)
                    if t == 3:
                        continue
                    for kh in range(2):
                        for t_ in (2, 3):
                            nm = ("ret_o", col, t_)
                            cols = slice((t_ - 2) * P, (t_ - 1) * P)

                            def emit(ps):
                                return product(ps, oH, oL, CHUNK_OF[("ret_o", 2 * col + kh)], cols, k0=KB * kh,
                                               start=kh == 0, stop=kh == 1)
                            if kh == 0:
                                last = tile(nm, emit, signal=False)
                                if t_ == 3:
                                    last.then_inc(half_k_used, 1)
                            else:
                                emit(bank_of(nm)).then_inc(psum_full, 1)
                elif kind == "attn_o":
                    _, c_, t = name
                    if name == ("attn_o", 0, 2):
                        pe.wait_ge(oL_ready, 6)
                    tile(name, lambda ps: product(ps, aH, aL, CHUNK_OF[("attn_o", c_)], slice((t - 2) * P, (t - 1) * P)))
                elif kind == "yT":
                    j = name[1]
                    pe.wait_ge(y_ready, 2 if j < 2 else 4)
                    tile(name, lambda ps: turn(ps, [gate_r[:, t, (2 * j + k) * P:(2 * j + k + 1) * P]
                                                    for k in range(2) for t in range(2)]))
                elif kind == "bc":
                    j = name[1]
                    if j == 0:
                        was_read(pe, ("ada", 11))
                        pe.wait_ge(in_mod2, 16)
                    tile(name, lambda ps: pe.matmul(ps[:], sel[:, 2:2 + P], mod2[:, j * CW:(j + 1) * CW],
                                                    start=True, stop=True))
                elif kind == "out":
                    _, c_, t = name
                    if name == ("out", 0, 2):
                        was_read(pe, ("yT", 3))
                    tile(name, lambda ps: product(ps, yH, yL, CHUNK_OF[("out", c_)], slice((t - 2) * P, (t - 1) * P)))
                elif kind == "h2T":
                    j = name[1]
                    pe.wait_ge(h2_ready, 2)
                    tile(name, lambda ps: turn(ps, [h2[:, t, (2 * j + k) * P:(2 * j + k + 1) * P]
                                                    for k in range(2) for t in range(2)]))
                elif kind == "logits":
                    was_read(pe, ("h2T", 3))
                    pe.wait_ge(in_late, 96)

                    def emit(ps):
                        for t in range(2):
                            for k in range(KB):
                                last = pe.matmul(ps[:, t * E:(t + 1) * E], h2T[:, k, t * P:(t + 1) * P], wr_sb[:, k, :],
                                                 start=k == 0, stop=k == KB - 1)
                        return last
                    tile(name, emit)
                elif kind == "rank":
                    pe.wait_ge(chosen_ready, 1)
                    pe.wait_ge(chain["pool"], 5 * RH + 1 - RH)

                    def emit(ps):
                        pe.matmul(ps[:, 0:E], tri[:], chosen[:, 0, :], start=True, stop=True)
                        pe.matmul(ps[:, E:2 * E], ones[:], chosen[:, 0, :], start=True, stop=False)
                        pe.matmul(ps[:, E:2 * E], tri[:], chosen[:, 1, :], start=False, stop=True)
                        pe.matmul(ps[:, 2 * E:3 * E], ones[:], chosen[:, 0, :], start=True, stop=False)
                        return pe.matmul(ps[:, 2 * E:3 * E], ones[:], chosen[:, 1, :], start=False, stop=True)
                    tile(name, emit)
                elif kind == "combT":
                    pe.wait_ge(comb_ready, 1)
                    tile(name, lambda ps: turn(ps, [comb[:, t, :] for t in range(2)]))

            was_read(pe, ("combT",))
            for t in range(2):
                for col in range(2):
                    pe.matmul(banks[2 * t + col][:], combT[:, t * P:(t + 1) * P], b2_sb[:, col * CW:(col + 1) * CW],
                              start=True, stop=False, skip_group_check=True)

            def gather(e):
                pe.wait_ge(onehot_ready, 2 * e + 2)
                for k in range(KB):
                    for part, rows_ in enumerate((h2H, h2L)):
                        cols = slice((k % 4) * P + part * CAP, (k % 4) * P + (part + 1) * CAP)
                        for t in range(2):
                            last = pe.matmul(banks[6 + k // 4][:, cols], rows_[:, t, k * P:(k + 1) * P],
                                             onehot[:, t, :], start=t == 0, stop=t == 1)
                last.then_inc(x_full, 1)

            def weights_times(ps, lhs, q, r):
                for k in range(KB):
                    m = 2 * q + k // 4
                    n = NPRE + m
                    if k % 4 == 0:
                        pe.wait_ge(l_ready, n + 1 + 12 * r)
                    pe.matmul(ps[:], lhs[:, k, :], wh[n % 4][:, k % 4, :], start=k == 0, stop=False)
                    last = pe.matmul(ps[:], lhs[:, k, :], wl[raw_count(m)[0]][:, k % 4, :],
                                     start=False, stop=k == KB - 1)
                    if k == 3:
                        last.then_inc(first_half_used, 1)
                last.then_inc(g_full, 1)

            def turn_first(e, i):
                pe.wait_ge(a_read, 4 * e + 4)
                if is_at(i, E - 1):
                    pe.wait_ge(tp_read, e)
                else:
                    pe.wait_ge(xg_ready, 2 * e + 4)
                for b in range(16):
                    ins = pe.matmul(banks[6 + b // 8][:, (b % 8) * CAP:(b % 8 + 1) * CAP],
                                    a_sb[:, b * P:(b + 1) * P], ident2[:], start=True, stop=True)
                ins.then_inc(t_full, 1)

            def scatter(e, stop=False):
                pe.wait_ge(o_read, 2 * e + 2)
                pe.wait_ge(tp_read, e + 1)
                for t in range(2):
                    for col in range(2):
                        ins = pe.matmul(banks[2 * t + col][:], spreadT[:, t * P:(t + 1) * P],
                                        out2[:, col * CW:(col + 1) * CW], start=False, stop=stop,
                                        skip_group_check=True)
                ins.then_inc(scattered, 1)

            def round_pe(i, p, q0, r):
                e = i + E * p
                first, last = is_at(i, 0), is_at(i, E)
                begun = not (first and is_at(p, FIRST_PASS))
                if first:
                    if begun:
                        pe.wait_ge(tp_read, e)
                    gather(e)
                jobs = (4, 5) if last else (0, 1, 2, 3) if first else range(6)
                for n, j in enumerate(jobs):
                    q = q0 + n
                    if last:
                        pe.wait_ge(o_read, 2 * (e - 2) + 1 + n)
                    elif j >= 2:
                        pe.wait_ge(a_read, 4 * e + j - 1)
                    elif is_at(i, 1):
                        pe.wait_ge(a_read, 4 * (e - 1) + 3 + j)
                    elif begun:
                        pe.wait_ge(o_read, (2 * e if first else 2 * (e - 1)) - 1 + j)
                    if j == 0:
                        pe.wait_ge(xg_ready, 2 * e + 2)
                    if j == 4:
                        pe.wait_ge(act_low, e)
                    weights_times(banks[4 + q % 2], xg if j < 4 else act_hl, q, r)
                    if n == 0 and not first and not is_at(i, 1):
                        scatter(e - 2)
                    if n == 1 and not first:
                        pe.wait_ge(spread_ready, 2 * e)
                        pe.wait_ge(t_read, 2 * e)
                        for t in range(2):
                            ins = pe.transpose(banks[6][:, t * P:(t + 1) * P], spread[:, t, :], ident[:])
                        ins.then_inc(tp_full, 1)
                    if j == 3 and not is_at(i, E - 1):
                        if not first:
                            pe.wait_ge(tp_read, e)
                        pe.wait_ge(xg_ready, 2 * e + 2)
                        gather(e + 1)
                    if j == 4 and not last:
                        turn_first(e, i)
                if first:
                    turn_first(e, i)
                if last:
                    scatter(e - 1, stop=True)

            was_read(pe, PLAN[-1][0])
            all_rounds(pe, round_pe)
            with more_passes(pe) as p:
                all_rounds(pe, round_pe, p)


def constants():
    import numpy as np

    m = np.zeros((P, C_END), np.float32)
    m[:, C_ID:C_ID + P] = np.eye(P)
    m[:, C_ID2:C_ID2 + CAP] = np.tile(np.eye(CAP), (2, 1))
    m[:, C_SLOT:C_SLOT + P] = np.arange(P) % CAP
    m[:, C_TRI:C_TRI + P] = np.triu(np.ones((P, P)), 1)
    row = np.arange(P)[:, None]
    for t in range(2):
        m[:, C_DIST + t * SEQ:C_DIST + (t + 1) * SEQ] = np.arange(SEQ)[None, :] - (row + t * P)
    m[0:5, C_SEL] = (1, 0, 1, 0, 1)
    m[0:5, C_SEL + 1] = (0, 1, 0, 1, 1)
    m[0:5, C_SEL + 2:C_SEL + 2 + P] = np.array([1, 0, 1, 0, 1])[:, None]
    for at, width in ((C_ROPER, RQK), (C_ROPEA, AD)):
        n = width // 4
        freq = (np.float32(10000.0) ** (-np.arange(n, dtype=np.float32) / np.float32(n))).astype(np.float32)
        for t in range(2):
            tok = np.arange(P) + t * P
            for axis, pos in enumerate((tok // 64, tok % 64)):
                ang = pos.astype(np.float32)[:, None] * freq
                for half in range(2):
                    o = at + t * width + (2 * axis + half) * n
                    m[:, o:o + n] = np.cos(ang)
                    m[:, o + 2 * width:o + 2 * width + n] = np.sin(ang) * (1 if half else -1)
    return m


_INS = ["x", "ctx", "norm2", "w_ada", "b_ada", "w_in", "ret_decay_f", "ret_decay_b", "attn_q_norm", "attn_k_norm",
        "w_ret_o", "w_attn_o", "w_out", "w_router", "b_router", "w_exp_in", "b_exp_in", "w_exp_out", "b_exp_out"]


def lay_out(inputs):
    import numpy as np

    arrays = {f"in_{name}": np.ascontiguousarray(inputs[name]) for name in _INS}
    columns = [np.asarray(inputs[name]).reshape(KB, P).T for name in ("c", "c_ctx", "norm1")]
    arrays["in_vectors"] = np.ascontiguousarray(np.concatenate(columns, axis=1))
    arrays["in_consts"] = constants()
    return arrays


def kernel(**inputs):
    import numpy as np
    import concourse.bacc as bacc
    from concourse.bass_utils import run_bass_kernel_spmd

    nc = bacc.Bacc("TRN2", target_bir_lowering=False, num_devices=1)
    arrays, args = lay_out(inputs), []
    for name, a in arrays.items():
        args.append(nc.dram_tensor(name, a.shape, mybir.dt.from_np(a.dtype), kind="ExternalInput").ap())
    args.append(nc.dram_tensor("out_0", (1, SEQ, D), mybir.dt.float32, kind="ExternalOutput").ap())
    hybrid_block(nc, *args)
    r = run_bass_kernel_spmd(nc, [arrays], core_ids=[0])
    return np.asarray(r.results[0]["out_0"])
```

```python
import concourse.bass as bass
from concourse import mybir
from contextlib import ExitStack, contextmanager

P = 128
D = 1024
KB = D // P
SEQ = 256
CTX = 256
RH, RQK, RV = 4, 256, 512
AH, AKV, AD = 8, 2, 128
E, FF, TOPK = 32, 1024, 4
CAP = 64
CW = 512
EPS = 1e-6
LIMIT, ALPHA = 7.0, 1.702

IN_COLS = {"qr": 0, "kr": 1024, "vr": 2048, "gr": 4096, "qa": 6144, "ka": 7168, "gate_r": 7680, "gate_a": 8704}

C_ID, C_ID2, C_SLOT, C_TRI, C_DIST, C_SEL = 0, 128, 192, 320, 448, 960
C_ROPER = C_SEL + 256
C_ROPEA = C_ROPER + 1024
C_END = C_ROPEA + 512


def chunks():
    out = [("ada", c, 0, c * CW) for c in range(4)]

    def w_in(kind, c):
        return (kind, c, 0, IN_COLS[kind] + c * CW)

    out += [w_in("qa", 0), w_in("qa", 1), w_in("ka", 0)]
    for pair in range(2):
        out += [w_in("qr", pair), w_in("kr", pair)]
        for h in (2 * pair, 2 * pair + 1):
            out += [w_in("vr", h), w_in("gr", h)]
    def ada(c):
        return ("ada", c, 0, c * CW)

    out += [w_in("gate_r", 0), w_in("gate_r", 1), ada(4), w_in("gate_a", 0), ada(5), w_in("gate_a", 1), ada(6)]
    for col in range(2):
        out += [("ret_o", 2 * col + kh, kh * D, col * CW) for kh in range(2)]
        out += [ada(7 + 2 * col)] + ([ada(8)] if col == 0 else [])
    out += [("attn_o", c, 0, c * CW) for c in range(2)] + [ada(11)]
    out += [("out", c, 0, c * CW) for c in range(2)] + [ada(10)]
    return out


CHUNKS = chunks()
NPRE = 2 * len(CHUNKS)
CHUNK_OF = {c[:2]: n for n, c in enumerate(CHUNKS)}
TILES_OF = {"qr": (2, 3), "kr": (0, 1, 2, 3), "vr": (0, 1, 2, 3), "gr": (2, 3), "qa": (2, 3),
            "ka": (0, 1, 2, 3), "gate_r": (2, 3), "gate_a": (2, 3)}


def psum_plan():
    plan = [(("ada", 0), "act")] + [(("xT", k), "act" if k % 2 else "dve") for k in range(KB)]
    plan += [(("ada", c), "act") for c in range(1, 4)] + [(("cols",), "dve")]
    reader = {"qr": "dve", "kr": "dve", "vr": "act", "gr": "dve", "qa": "act", "ka": "act",
              "gate_r": "act", "gate_a": "act"}
    after = {}
    s = 0
    slots = []
    for kind, c, _, _ in CHUNKS:
        if kind in reader:
            for t in TILES_OF[kind]:
                slots.append((kind, c, t))
                if kind in ("qa", "ka", "qr", "kr"):
                    after.setdefault(s + 2, []).append((("rT", kind, c, t), "act"))
                s += 1

    def at(n, name, who):
        after.setdefault(n, []).append((name, who))

    first = slots.index(("qr", 0, 2)) + 2
    for u in range(2 * AH):
        n = first + u
        at(n, ("score", u // 2, u % 2), "act")
        at(n + 2, ("pT", u // 2, u % 2), "act")
        if u % 2:
            at(n + 3, ("av", u // 2), "dve")

    at(slots.index(("gate_r", 1, 3)), ("ada", 4), "act")
    at(slots.index(("gate_a", 0, 3)), ("ada", 5), "act")
    at(slots.index(("gate_a", 1, 3)), ("ada", 6), "act")
    for h in range(RH):
        v_end, g_end = slots.index(("vr", h, 3)), slots.index(("gr", h, 3))
        at(v_end, ("rs", h, 0), "dve")
        at(v_end, ("rs", h, 1), "dve")
        at(g_end, ("ro", h, 0), "dve")
        at(g_end, ("ro", h, 1), "dve")
        at(g_end + (4 if h == 0 else 3), ("oT", h, 0), "act")
        at(g_end + (4 if h == 0 else 3), ("oT", h, 1), "act")
    for n, (kind, c, t) in enumerate(slots):
        plan.append((("proj", kind, c, t), reader[kind]))
        order = {"ada": 9, "rT": -1, "av": 0, "pT": 1, "score": 3}
        plan += sorted(after.get(n, []), key=lambda x: order.get(x[0][0], 4))
    plan += [(("ret_o", 0, t), "dve") for t in (2, 3)]
    plan += [(("ada", 7), "act"), (("ada", 8), "act")]
    plan += [(("ret_o", 1, t), "dve") for t in (2, 3)]
    plan += [(("b1", 0), "act"), (("ada", 9), "act")]
    plan += [(("attn_o", c, t), "dve") for c in range(2) for t in (2, 3)]
    plan += [(("ada", 11), "act")]
    plan += [(("yT", j), "dve") for j in range(4)]
    plan += [(("bc", j), "act") for j in range(6)]
    plan += [(("out", c, t), "dve") for c in range(2) for t in (2, 3)]
    plan += [(("ada", 10), "act")]
    plan += [(("h2T", j), "act") for j in range(4)]
    plan += [(("logits",), "dve"), (("bc", 6), "act"), (("bc", 7), "act")]
    plan += [(("rank",), "dve"), (("combT",), "dve")]
    return plan


PLAN = psum_plan()
TILE_AT = {name: n for n, (name, _) in enumerate(PLAN)}
READ_AT = {}
for _n, (_name, _who) in enumerate(PLAN):
    READ_AT[_name] = 1 + sum(w == _who for _, w in PLAN[:_n])


def hybrid_block(nc, x, ctx_in, norm2, w_ada, b_ada, w_in, decay_f, decay_b, q_norm,
                 k_norm, w_ret_o, w_attn_o, w_out, w_router, b_router, w1, b1, w2, b2, vectors, consts, out):
    f32, f32r = mybir.dt.float32, mybir.dt.float32r
    ALU, ACT, AX = mybir.AluOpType, mybir.ActivationFunctionType, mybir.AxisListType
    stack = ExitStack()
    with stack:
        base = -(-nc.sbuf_base // 32) * 32
        size = (nc.sbuf_usable_end - base) // 4 // 8 * 8
        stack.enter_context(nc.sbuf_tensor("slab", [P, (nc.sbuf_usable_end - base) // 4 - 8], f32))

        def at(name, kib, shape, dtype=f32, extra=0):
            n = 1
            for s in shape[1:]:
                n *= s
            assert kib * 1024 + extra + 4 * n <= 4 * size, name
            return nc.alloc_sbuf_tensor_at(name, shape, dtype, offset=base + int(kib * 1024) + extra)

        raw = [at(f"raw{s}", 8 * s, [P, 4, CW]) for s in range(8)]
        wl = [at(f"wl{s}", 8 * s, [P, 4, CW], f32r) for s in range(8)]
        wh = [at(f"wh{s}", 64 + 8 * s, [P, 4, CW], f32r) for s in range(4)]
        hH = at("hH", 96, [P, KB, 512], f32r)
        hL = at("hL", 112, [P, KB, 512], f32r)
        silu_c = at("silu_c", 128, [P, KB, P], f32r)
        F = 132
        rows = at("rows", F, [P, 4, D])
        xT = at("xT", F + 16, [P, KB, 512])
        mod1 = at("mod1", F + 32, [5, 2048])
        qaT = at("qaT", F, [P, AH, SEQ])
        kaT = at("kaT", F + 8, [P, AKV, 512])
        va = at("va", F + 12, [P, 4, AKV * AD])
        prob = [at(f"prob{s}", F + 16 + 2 * s, [P, 512]) for s in range(2)]
        junk_q = at("junk_q", F + 44, [P, 512])
        probT = at("probT", F + 20, [P, 4, SEQ])
        oaT = at("oaT", F + 24, [P, AH, SEQ])
        oT = at("oT", F, [P, RH * 4, SEQ])
        qrT = at("qrT", F + 32, [P, 4, SEQ])
        krT = at("krT", F + 36, [P, 4, 512])
        v = at("v", F + 44, [P, 4, RV])
        g = at("g", F + 52, [P, 2, RV])
        decay = at("decay", F + 56, [P, 4, SEQ])
        decay2 = at("decay2", F + 60, [P, 512])
        roped = [at(f"roped{s}", F + 62 + 2 * s, [P, 512]) for s in range(2)]
        ropes = at("ropes", F + 66, [P, 512])
        rope_r = at("rope_r", F + 68, [P, 2, 2, 256])
        rope_a = at("rope_a", F + 56, [P, 2, 2, 128])
        gains = at("gains", F + 58, [P, 2, 128])
        dist = at("dist", F + 72, [P, 2, SEQ])
        gate_r = at("gate_r", F + 32, [P, 2, D])
        gate_a = at("gate_a", F + 40, [P, 2, D])
        mod2 = at("mod2", F + 48, [5, 3072])
        mod_g2 = at("mod_g2", 112, [5, D])
        oH = at("oH", 96, [P, RH * 4, SEQ], f32r)
        oL = at("oL", 112, [P, RH * 4, SEQ], f32r)
        aH = at("aH", F, [P, AH, SEQ], f32r)
        aL = at("aL", F + 8, [P, AH, SEQ], f32r)
        yH = at("yH", F + 16, [P, KB, SEQ], f32r)
        yL = at("yL", F + 24, [P, KB, SEQ], f32r)
        x1 = at("x1", F + 64, [P, 2, D])
        bc = at("bc", F + 32, [P, 4, D])
        norm2_b = at("norm2_b", 124, [P, D])
        h2 = at("h2", F, [P, 2, D])
        h2T = at("h2T", F + 8, [P, KB, SEQ])
        for s, kib in enumerate((F + 24, F + 32, F + 48, F + 56)):
            raw.append(at(f"raw{8 + s}", kib, [P, 4, CW]))
            wl.append(at(f"wl{8 + s}", kib, [P, 4, CW], f32r))
        h2H = at("h2H", 96, [P, 2, D], f32r)
        h2L = at("h2L", 104, [P, 2, D], f32r)
        xg = at("xg", 112, [P, KB, P], f32r)
        b2_sb = at("b2_sb", 128, [E, D])
        act_hl = at("act_hl", 116, [P, KB, P], f32r)
        wr_sb = at("wr_sb", 116, [P, KB, E])
        onehot = at("onehot", 120, [P, 2, CAP], f32r)
        ident2 = at("ident2", 120, [P, CAP], extra=512)
        slot_no = at("slot_no", 120, [P, P], extra=768)
        tri = at("tri", 120, [P, P], extra=1280)
        ones = at("ones", 120, [P, P], extra=1792)
        br_b = at("br_b", 120, [P, E], extra=2304)
        a_sb = at("a_sb", F, [P, 2 * FF])
        out2 = at("out2", F + 8, [P, D])
        gate = at("gate", F + 12, [P, 512])
        sig = at("sig", F + 14, [P, 512])
        up = at("up", F + 16, [P, 512])
        spread = at("spread", F + 18, [P, 2, P])
        spreadT = at("spreadT", F + 19, [P, SEQ])
        lp = at("lp", F + 20, [P, 2, 40])
        lm = at("lm", F + 20, [P, 2, 40], extra=320)
        top = at("top", F + 20, [P, 2, 8], extra=640)
        rep = at("rep", F + 20, [P, 2, 8], extra=704)
        chosen = at("chosen", F + 20, [P, 2, E], extra=768)
        comb = at("comb", F + 21, [P, 2, E])
        rank = at("rank", F + 21, [P, 2, E], extra=256)
        route = at("route", F + 21, [P, 16], extra=512)
        now_rank = at("now_rank", F + 21, [P, 2, 1], extra=576)
        own_rank = at("own_rank", F + 21, [P, 2, 1], extra=608)
        own_comb = at("own_comb", F + 21, [P, 2, 1], extra=640)
        most = at("most", F + 21, [P, 1], extra=672)
        most_int = at("most_int", F + 21, [P, 1], mybir.dt.int32, extra=704)
        combT = at("combT", F + 22, [E, SEQ])
        junk2 = at("junk2", F + 8, [P, D])
        b1_rows = at("b1_rows", F + 16, [E, 2 * FF])
        b1_cols = at("b1_cols", F + 72, [P, 16, E])
        ident = at("ident", F + 74, [P, P])
        sel = at("sel", F + 74, [5, 2 + P], extra=512)
        stat = at("stat", F + 74, [P, 32], extra=1056)
        logdec = at("logdec", F + 74, [P, 2 * RH], extra=1184)
        lowdec = at("lowdec", F + 74, [P, 2 * RH], extra=1216)
        decin = at("decin", F + 74, [P, 2 * RH], extra=1248)
        cols_in = at("cols_in", F + 40, [P, 3, KB])
        cc = at("cc", F + 40, [P, KB, 2], extra=96)
        scale1 = at("scale1", F + 41, [P, KB, 2])
        shift1 = at("shift1", F + 41, [P, KB, 2], extra=64)

        banks = [stack.enter_context(nc.psum_tensor(f"bank{b}", [P, 512], f32)) for b in range(8)]

        def sem(name):
            return stack.enter_context(nc.semaphore(name))

        raw_in = [sem(f"raw_in{s}") for s in range(12)]
        first_half_used = sem("first_half_used")
        h_ready, l_ready = sem("high_half_ready"), sem("low_half_ready")
        psum_full = sem("psum_full")
        read = {"act": sem("psum_read_by_act"), "dve": sem("psum_read_by_dve")}
        half_k_used = sem("half_k_used")
        in_ident, in_rows, in_cols = sem("in_ident"), sem("in_rows"), sem("in_cols")
        in_tables, in_decay, in_bada = sem("in_tables"), sem("in_decay"), sem("in_b_ada")
        in_x1, in_mod2, in_b1, in_late = sem("in_x1"), sem("in_mod2"), sem("in_b1"), sem("in_late")
        in_norm2, in_b2 = sem("in_norm2"), sem("in_b2")
        squares = sem("squares_summed")
        var_ready, std_ready = sem("var_ready"), sem("std_ready")
        normed, silu_ready, sigm = sem("rows_normed"), sem("silu_c_ready"), sem("sigmoid_of_c")
        h_rounded, h_split = sem("h_rounded"), sem("h_split")
        h_full = sem("h_modulated")
        hc_full, hc_rounded, hc_split = sem("context_modulated"), sem("context_rounded"), sem("context_split")
        roped_ready, neg_max, prob_ready = sem("roped_ready"), sem("neg_max"), sem("prob_ready")
        exponent, exp_done, decay_ready = sem("exponent_ready"), sem("decay_exps"), sem("decay_ready")
        dec_abs, dec_ready = sem("softplus_parts"), sem("log_decay_ready")
        sg_ready = sem("sigmoid_g")
        oH_ready, oL_ready = sem("o_rounded"), sem("o_split")
        y_ready, yH_ready = sem("y_ready"), sem("y_rounded")
        x1_ready, h2_ready = sem("x1_ready"), sem("h2_ready")
        h2_rounded, h2_split = sem("h2_rounded"), sem("h2_split")
        expl, chosen_ready, comb_ready = sem("exp_logits"), sem("chosen_ready"), sem("comb_ready")
        neg_top, rank_ready = sem("neg_top"), sem("rank_ready")
        g_full, a_read, o_read = sem("chunk_full"), sem("first_read"), sem("second_read")
        x_full, xg_ready = sem("gather_full"), sem("gather_read")
        onehot_ready, spread_ready = sem("onehot_ready"), sem("spread_ready")
        tp_full, tp_read = sem("spreadT_full"), sem("spreadT_read")
        t_full, t_read = sem("turned_full"), sem("turned_read")
        scattered, half_scattered = sem("scattered"), sem("half_scattered")
        clipped, sig_ready = sem("gate_clipped"), sem("sigmoid_gate")
        act_ready, act_high, act_low = sem("act_ready"), sem("act_high"), sem("act_low")
        most_ready = sem("most_tokens_ready")
        shifted, up_steps, columns_ready = sem("rank_shifted"), sem("up_steps"), sem("columns_ready")
        y_out, out_done = sem("y_out"), sem("out_done")
        chain = {n: sem(f"{n}_step") for n in ("act", "dve", "pool")}

        weights = {"ada": w_ada, "ret_o": w_ret_o, "attn_o": w_attn_o, "out": w_out}

        def half_source(n):
            kind, _, row, col = CHUNKS[n // 2]
            w = weights.get(kind, w_in)
            r = row + 512 * (n % 2)
            return w[0, r:r + 512, col:col + CW].rearrange("(k p) n -> p k n", p=P)

        FIRST_PASS = 0
        PLACES = (6, 7, 0, 1, 10, 11, 2, 3, 4, 5, 8, 9)
        assert NPRE % 8 == 6
        BEFORE = [sum(1 for n in range(NPRE) if n % 8 == s) for s in range(8)] + [0] * 4

        def raw_count(m):
            s = PLACES[m % 12]
            return s, 16 * (BEFORE[s] + m // 12 + 1)

        def chunk_released(n):
            kind, c, _, _ = CHUNKS[n]
            if kind == "ret_o":
                if c % 2 == 0:
                    return half_k_used, c // 2 + 1
                return psum_full, TILE_AT[("ret_o", c // 2, 3)] + 1
            if kind == "ada":
                return psum_full, TILE_AT[("ada", c)] + 1
            if kind in ("attn_o", "out"):
                return psum_full, TILE_AT[(kind, c, 3)] + 1
            return psum_full, TILE_AT[("proj", kind, c, 3)] + 1

        FIRST_TILE = {}
        for n_, (kind, c_, _, _) in enumerate(CHUNKS):
            if kind == "ada":
                FIRST_TILE.setdefault(TILE_AT[("ada", c_)], []).append(n_)
            elif kind == "ret_o":
                FIRST_TILE.setdefault(TILE_AT[("ret_o", c_ // 2, 2)], []).append(n_)
            elif kind in ("attn_o", "out"):
                FIRST_TILE.setdefault(TILE_AT[(kind, c_, 2)], []).append(n_)
            else:
                FIRST_TILE.setdefault(TILE_AT[("proj", kind, c_, TILES_OF[kind][0])], []).append(n_)

        def bank_of(name):
            return banks[TILE_AT[name] % 8]

        def full(eng, name):
            eng.wait_ge(psum_full, TILE_AT[name] + 1)

        def was_read(eng, name):
            eng.wait_ge(read[PLAN[TILE_AT[name]][1]], READ_AT[name])

        class Steps:

            def __init__(self, eng, which, start=0):
                self.eng, self.sem, self.n, self.add = eng, chain[which], start, 0

            def link(self, ins):
                self.n += 1
                ins.then_inc(self.sem, 1)
                self.eng.wait_ge(self.sem, self.add + self.n)

        ROPED = [x[0] for x in PLAN if x[0][0] == "rT"]

        def plain(r):
            return ROPED[r][1] == "kr" and ROPED[r][3] < 2

        def in_roped(eng, r):
            if plain(r):
                was_read(eng, ("proj",) + ROPED[r][1:])
            else:
                eng.wait_ge(roped_ready, sum(not plain(j) for j in range(r + 1)))

        def all_rounds(eng, round_, p=0):
            round_(0, p, 0, E * p)
            round_(1, p, 4, E * p)
            with eng.Fori(2, E - 1) as i:
                round_(i, p, 4, E * p + (i - 1))
            round_(E - 1, p, 4 + 6 * (E - 2), E * p)
            round_(E, p, 4 + 6 * (E - 1), E * p)

        def is_at(i, n):
            return isinstance(i, int) and i == n

        @contextmanager
        def more_passes(eng):
            eng.wait_ge(most_ready, 1)
            count = eng.value_load(most_int[0:1, 0:1], min_val=0, max_val=SEQ)
            with eng.If(count > CAP):
                with eng.Fori(1, SEQ // CAP) as p:
                    yield p

        block = stack.enter_context(nc.Block())

        @block.sync
        def _(sp):
            def load(n):
                if n >= 8:
                    sp.wait_ge(*chunk_released(n // 2 - 4))
                sp.dma_start(raw[n % 8][:], half_source(n)).then_inc(raw_in[n % 8], 16)

            sp.dma_start(cols_in[:].rearrange("p a k -> p (a k)"), vectors).then_inc(in_cols, 16)
            load(0)
            load(1)
            sp.dma_start(ident[:], consts[:, C_ID:C_ID + P]).then_inc(in_ident, 16)
            sp.dma_start(rows[:, 2:4, :], x[0].rearrange("(t p) d -> p t d", p=P)).then_inc(in_rows, 16)
            sp.dma_start(rows[:, 0:2, :], ctx_in[0].rearrange("(t p) d -> p t d", p=P)).then_inc(in_rows, 16)
            sp.dma_start(sel[:], consts[0:5, C_SEL:C_SEL + 2 + P]).then_inc(in_ident, 16)
            sp.dma_start(mod1[4:5, :], b_ada[:, 0:2048]).then_inc(in_bada, 16)
            for n in range(2, 8):
                load(n)
            sp.dma_start(rope_r[:], consts[:, C_ROPER:C_ROPER + 1024]
                         .rearrange("p (a t f) -> p a t f", a=2, t=2)).then_inc(in_tables, 16)
            sp.dma_start(rope_a[:], consts[:, C_ROPEA:C_ROPEA + 512]
                         .rearrange("p (a t f) -> p a t f", a=2, t=2)).then_inc(in_tables, 16)
            sp.dma_start(gains[:, 0, :], q_norm[0:1, :].broadcast_to([P, AD])).then_inc(in_tables, 16)
            sp.dma_start(gains[:, 1, :], k_norm[0:1, :].broadcast_to([P, AD])).then_inc(in_tables, 16)
            sp.dma_start(dist[:], consts[:, C_DIST:C_DIST + 512]
                         .rearrange("p (t f) -> p t f", t=2)).then_inc(in_tables, 16)
            sp.dma_start(decin[:, 0:RH], decay_f[0:1, :].broadcast_to([P, RH])).then_inc(in_decay, 16)
            sp.dma_start(decin[:, RH:2 * RH], decay_b[0:1, :].broadcast_to([P, RH])).then_inc(in_decay, 16)
            x1_at = 2 * CHUNK_OF[("vr", 3)]
            mod2_at = 2 * CHUNK_OF[("ada", 5)]
            for n in range(8, NPRE):
                load(n)
                if n == x1_at:
                    full(sp, ("rT", "kr", 1, 3))
                    sp.dma_start(x1[:], x[0].rearrange("(t p) d -> p t d", p=P)).then_inc(in_x1, 16)
                if n == mod2_at:
                    full(sp, ("oT", RH - 1, 1))
                    sp.wait_ge(read["dve"], READ_AT[("ro", RH - 1, 1)])
                    sp.dma_start(mod2[4:5, :], b_ada[:, 2048:5120]).then_inc(in_mod2, 16)
                    sp.dma_start(b1_rows[:], b1[0]).then_inc(in_b1, 16)

            full(sp, ("ret_o", 1, 3))
            sp.dma_start(norm2_b[:], norm2[0:1, :].broadcast_to([P, D])).then_inc(in_norm2, 16)
            sp.dma_start(mod_g2[4:5, :], b_ada[:, 5120:6144]).then_inc(in_late, 16)
            sp.dma_start(wr_sb[:], w_router[0].rearrange("(k p) e -> p k e", p=P)).then_inc(in_late, 16)
            sp.dma_start(ident2[:], consts[:, C_ID2:C_ID2 + CAP]).then_inc(in_late, 16)
            sp.dma_start(slot_no[:], consts[:, C_SLOT:C_SLOT + P]).then_inc(in_late, 16)
            sp.dma_start(tri[:], consts[:, C_TRI:C_TRI + P]).then_inc(in_late, 16)
            sp.dma_start(br_b[:], b_router[0:1, :].broadcast_to([P, E])).then_inc(in_late, 16)

            def expert_half(m, src, r):
                s, _ = raw_count(m)
                if isinstance(r, int) and m < 12:
                    if s < 8:
                        sp.wait_ge(*chunk_released((NPRE - 8 + (s - NPRE) % 8) // 2))
                    elif s < 10:
                        sp.wait_ge(h2_split, 2)
                        if m % 2 == 0:
                            full(sp, ("ada", 10))
                            sp.dma_start(b2_sb[:], b2[0]).then_inc(in_b2, 16)
                    elif s == 10:
                        full(sp, ("bc", 5))
                else:
                    sp.wait_ge(g_full if m % 2 else first_half_used, m // 2 - 5 + 6 * r)
                sp.dma_start(raw[s][:], src).then_inc(raw_in[s], 16)

            def w1_half(e, j):
                return w1[0, e, 512 * (j % 2):512 * (j % 2) + 512, CW * (j // 2):CW * (j // 2) + CW] \
                    .rearrange("(k p) n -> p k n", p=P)

            def w2_half(e, j):
                return w2[0, e, 512 * (j % 2):512 * (j % 2) + 512, CW * (j // 2):CW * (j // 2) + CW] \
                    .rearrange("(k p) n -> p k n", p=P)

            def round_(i, p, q0, r):
                if not is_at(i, E):
                    for j in range(8):
                        expert_half(2 * q0 + j, w1_half(i, j), r)
                if not is_at(i, 0):
                    for j in range(4):
                        expert_half(2 * q0 + (0 if is_at(i, E) else 8) + j, w2_half(i - 1, j), r)

            all_rounds(sp, round_)
            with more_passes(sp) as p:
                all_rounds(sp, round_, p)
            for col in range(2):
                cols = slice(col * CW, (col + 1) * CW)
                sp.wait_ge(out_done, col + 1)
                sp.dma_start(out[0, :, cols].rearrange("(t p) d -> p t d", p=P), x1[:, :, cols]).then_inc(y_out, 16)
            sp.wait_ge(y_out, 32)

        @block.scalar
        def _(act):
            st = Steps(act, "act")

            def split_high(n):
                act.wait_ge(raw_in[n % 8], 16 * (n // 8 + 1))
                if n >= 4:
                    act.wait_ge(*chunk_released(n // 2 - 2))
                act.activation(wh[n % 4][:], raw[n % 8][:], ACT.Copy).then_inc(h_ready, 1)

            def done(ins):
                ins.then_inc(read["act"], 1)

            def expert_half_split(m, p, r):
                s, count = raw_count(m)
                q = m // 2
                act.wait_ge(raw_in[s], count + 16 * r)
                if is_at(p, FIRST_PASS) and q < 2:
                    act.wait_ge(*chunk_released(len(CHUNKS) - 2 + q))
                else:
                    act.wait_ge(g_full if m % 2 else first_half_used, q - 1 + 6 * r)
                act.activation(wh[(NPRE + m) % 4][:], raw[s][:], ACT.Copy).then_inc(h_ready, 1)

            def expert_split(q, p, r):
                expert_half_split(2 * q, p, r)
                expert_half_split(2 * q + 1, p, r)

            stds = [0]

            def std(col, n):
                stds[0] += 1
                act.wait_ge(var_ready, stds[0])
                act.activation(stat[:, col + n:col + 2 * n], stat[:, col:col + n], ACT.Sqrt).then_inc(std_ready, 1)

            act.wait_ge(in_cols, 16)
            act.activation(cc[:].rearrange("p k s -> p s k"), cols_in[:, 0:2, :], ACT.Sigmoid).then_inc(sigm, 1)
            split_high(0)
            split_high(1)
            act.wait_ge(in_rows, 32)
            for t in range(4):
                act.activation(xT[:, 2 * t:2 * t + 2, :].rearrange("p a b -> p (a b)"), rows[:, t, :], ACT.Square,
                               accum_out=stat[:, t:t + 1]).then_inc(squares, 1)
            std(0, 4)

            for n, (name, reader) in enumerate(PLAN):
                for chunk in FIRST_TILE.get(n, []):
                    if chunk + 1 < len(CHUNKS):
                        split_high(2 * chunk + 2)
                        split_high(2 * chunk + 3)
                kind = name[0]
                if name[:2] == ("proj", "vr") and name[3] == 0:
                    h = name[2]
                    act.wait_ge(exponent, h + 1)
                    act.activation(decay[:, 2:4, :], decay[:, 2:4, :], ACT.Exp).then_inc(exp_done, 1)
                    act.activation(decay[:, 0:2, :], dist[:], ACT.Exp, scale=logdec[:, h:h + 1],
                                   bias=lowdec[:, h:h + 1]).then_inc(exp_done, 1)
                    act.activation(decay2[:].rearrange("p (a b) -> p a b", b=SEQ), dist[:], ACT.Exp,
                                   scale=decin[:, RH + h:RH + h + 1],
                                   bias=lowdec[:, RH + h:RH + h + 1]).then_inc(exp_done, 1)
                if kind == "xT" and reader == "act":
                    full(act, name)
                    done(act.activation(xT[:, name[1], :], bank_of(name)[:], ACT.Copy))
                elif kind == "ada":
                    j = name[1]
                    rows_, at_ = (mod1, 0) if j < 4 else (mod2, 4) if j < 10 else (mod_g2, 10)
                    dst = rows_[0:4, (j - at_) * CW:(j - at_ + 1) * CW]
                    full(act, name)
                    done(act.activation(dst, bank_of(name)[0:4, :], ACT.Copy))
                elif kind == "cols":
                    for k in range(KB):
                        act.wait_ge(h_full, k + 1)
                        act.activation(hH[:, k, CTX:], xT[:, k, CTX:], ACT.Copy).then_inc(h_rounded, 1)
                elif kind == "proj":
                    _, w, c_, t = name
                    if w in ("qa", "ka"):
                        r = ROPED.index(("rT", w, c_, t))
                        if r >= 2:
                            full(act, ROPED[r - 2])
                        full(act, name)
                        heads = 4 if w == "qa" else 2
                        act.activation(roped[r % 2][:, 0:heads * AD], bank_of(name)[:, 0:heads * AD], ACT.Copy)
                        if w == "ka":
                            act.activation(va[:, t, :], bank_of(name)[:, 256:512], ACT.Copy)
                        if r:
                            in_roped(act, r - 1)
                        for j in range(heads):
                            ins = act.activation(junk_q[:, j * AD:(j + 1) * AD], bank_of(name)[:, j * AD:(j + 1) * AD],
                                                 ACT.Square, accum_out=stat[:, 8 + j:9 + j])
                        done(ins)
                        std(8, heads)
                    elif w == "vr":
                        full(act, name)
                        done(act.activation(v[:, t, :], bank_of(name)[:], ACT.Copy))
                    elif w == "gr":
                        full(act, name)
                        act.activation(g[:, t - 2, :], bank_of(name)[:], ACT.Sigmoid).then_inc(sg_ready, 1)
                    elif w in ("gate_r", "gate_a"):
                        dst = gate_r if w == "gate_r" else gate_a
                        full(act, name)
                        done(act.activation(dst[:, t - 2, c_ * CW:(c_ + 1) * CW], bank_of(name)[:], ACT.Sigmoid))
                elif kind == "rT":
                    _, w, c_, t = name
                    full(act, name)
                    src = bank_of(name)[:].rearrange("p (a b) -> p a b", b=P)
                    if w == "qa":
                        dst = qaT[:, 4 * c_:4 * c_ + 4, (t - 2) * P:(t - 1) * P]
                    elif w == "ka":
                        dst, src = kaT[:, :, t * P:(t + 1) * P], src[:, 0:2, :]
                    elif w == "qr":
                        dst = qrT[:, :, (t - 2) * P:(t - 1) * P]
                    else:
                        dst = krT[:, :, t * P:(t + 1) * P]
                    done(act.activation(dst, src, ACT.Copy))
                elif kind == "score":
                    _, h, t = name
                    u = 2 * h + t
                    full(act, name)
                    act.wait_ge(neg_max, u + 1)
                    if u >= 2:
                        full(act, ("pT", (u - 2) // 2, (u - 2) % 2))
                    done(act.activation(prob[u % 2][:], bank_of(name)[:], ACT.Exp, scale=AD ** -0.5,
                                        bias=stat[:, 24 + u % 2:25 + u % 2], accum_out=stat[:, 26 + u % 2:27 + u % 2]))
                elif kind == "pT":
                    _, h, t = name
                    full(act, name)
                    if h:
                        full(act, ("av", h - 1))
                    done(act.activation(probT[:, :, t * P:(t + 1) * P],
                                        bank_of(name)[:].rearrange("p (a b) -> p a b", b=P), ACT.Copy))
                elif kind == "ro":
                    _, h, t = name
                    full(act, name)
                    act.wait_ge(decay_ready, h + 1)
                    act.wait_ge(squares, 4 + 2 * h + t)
                    act.activation(decay2[:], bank_of(name)[:], ACT.Square,
                                   accum_out=stat[:, 16 + t:17 + t]).then_inc(squares, 1)
                    if t == 1:
                        std(16, 2)
                elif kind == "oT":
                    _, h, b = name
                    full(act, name)
                    done(act.activation(oT[:, 4 * h + 2 * b:4 * h + 2 * b + 2, :],
                                        bank_of(name)[:].rearrange("p (a b) -> p a b", b=SEQ), ACT.Copy))
                elif kind == "b1":
                    full(act, name)
                    act.activation(b1_cols[:, 0:8, :], bank_of(name)[:, 0:8 * E].rearrange("p (a b) -> p a b", b=E),
                                   ACT.Copy)
                    done(act.activation(b1_cols[:, 8:16, :], bank_of(name)[:, 8 * E:16 * E]
                                        .rearrange("p (a b) -> p a b", b=E), ACT.Copy, bias=1.0))
                elif kind == "yT":
                    full(act, name)
                    j = name[1]
                    act.activation(yH[:, 2 * j:2 * j + 2, :], bank_of(name)[:].rearrange("p (a b) -> p a b", b=SEQ),
                                   ACT.Copy).then_inc(yH_ready, 1)
                elif kind == "bc":
                    full(act, name)
                    j = name[1]
                    done(act.activation(bc[:, j // 2, (j % 2) * CW:(j % 2 + 1) * CW], bank_of(name)[:], ACT.Copy))
                elif kind == "h2T":
                    full(act, name)
                    j = name[1]
                    done(act.activation(h2T[:, 2 * j:2 * j + 2, :], bank_of(name)[:].rearrange("p (a b) -> p a b", b=SEQ),
                                        ACT.Copy))
                if name == ("proj", "qa", 0, 2):
                    was_read(act, ("cols",))
                    was_read(act, ("xT", KB - 2))
                    was_read(act, ("xT", KB - 1))
                    for k in range(KB):
                        act.activation(xT[:, k, 0:CTX], xT[:, k, 0:CTX], ACT.Identity, scale=scale1[:, k, 1:2],
                                       bias=shift1[:, k, 1:2]).then_inc(hc_full, 1)
                    for k in range(KB):
                        act.wait_ge(hc_full, k + 1)
                        act.activation(hH[:, k, 0:CTX], xT[:, k, 0:CTX], ACT.Copy).then_inc(hc_rounded, 1)
                if name == ("proj", "qa", 1, 3):
                    act.wait_ge(in_decay, 32)
                    st.link(act.activation(lowdec[:], decin[:], ACT.Abs))
                    st.link(act.activation(lowdec[:], lowdec[:], ACT.Exp, scale=-1.0))
                    act.activation(lowdec[:], lowdec[:], ACT.Ln, bias=1.0).then_inc(dec_abs, 1)
                if name in (("proj", "gate_a", 1, 3), ("ada", 6)):
                    for j in (0, 1) if kind == "proj" else (2, 3):
                        act.activation(oH[:, 4 * j:4 * j + 4, :], oT[:, 4 * j:4 * j + 4, :], ACT.Copy).then_inc(oH_ready, 1)
                if name == ("ret_o", 0, 3):
                    act.wait_ge(oL_ready, 4)
                    for j in range(2):
                        act.activation(aH[:, 4 * j:4 * j + 4, :], oaT[:, 4 * j:4 * j + 4, :], ACT.Copy).then_inc(oH_ready, 1)
                if name[:2] == ("out", 1):
                    t = name[2] - 2
                    act.wait_ge(x1_ready, t + 1)
                    act.wait_ge(squares, 4 + 2 * RH + t)
                    act.activation(junk2[:], x1[:, t, :], ACT.Square, accum_out=stat[:, 2 * t:2 * t + 1]) \
                        .then_inc(squares, 1)
                    std(2 * t, 1)
                    if t:
                        expert_half_split(0, FIRST_PASS, 0)
                if name == ("h2T", 3):
                    for t in range(2):
                        act.wait_ge(h2_ready, t + 1)
                        act.activation(h2H[:, t, :], h2[:, t, :], ACT.Copy).then_inc(h2_rounded, 1)
                if name == ("logits",):
                    for t in range(2):
                        act.wait_ge(neg_top, t + 1)
                        act.activation(comb[:, t, :], lp[:, t, 0:E], ACT.Exp, bias=route[:, t:t + 1]).then_inc(expl, 1)
                    expert_half_split(1, FIRST_PASS, 0)
                    expert_split(1, FIRST_PASS, 0)

            def gather_read(e):
                act.wait_ge(x_full, e + 1)
                for k in range(2):
                    act.activation(xg[:, 4 * k:4 * k + 4, :], banks[6 + k][:].rearrange("p (a b) -> p a b", b=P),
                                   ACT.Copy).then_inc(xg_ready, 1)

            def sigmoid_of_gate(e):
                act.wait_ge(clipped, e)
                act.activation(sig[:], gate[:], ACT.Sigmoid, scale=ALPHA).then_inc(sig_ready, 1)

            def act_rounded(i, e, p):
                act.wait_ge(act_ready, e)
                if not (is_at(i, 1) and is_at(p, FIRST_PASS)):
                    act.wait_ge(o_read, 2 * (e - 1))
                act.activation(act_hl[:, :, 0:CAP], gate[:].rearrange("p (k c) -> p k c", c=CAP),
                               ACT.Copy).then_inc(act_high, 1)

            def round_act(i, p, q0, r):
                e = i + E * p
                first, last = is_at(i, 0), is_at(i, E)
                if first:
                    if not is_at(p, FIRST_PASS):
                        expert_split(0, p, r)
                    gather_read(e)
                if last:
                    sigmoid_of_gate(e)
                    expert_half_split(2 * q0 + 2, p, r)
                    act_rounded(i, e, p)
                    expert_half_split(2 * q0 + 3, p, r)
                    return
                for n, j in enumerate((0, 1, 2, 3) if first else range(6)):
                    q = q0 + n
                    if not (first and n == 0 and is_at(p, FIRST_PASS)):
                        expert_split(q + 1, p, r)
                    if n == 4 and not is_at(i, E - 1):
                        gather_read(e + 1)
                    if j < 4:
                        act.wait_ge(g_full, q + 1 + 6 * r)
                        if j == 0 and not (first and is_at(p, FIRST_PASS)):
                            act.wait_ge(t_full, e)
                        act.activation(a_sb[:, j * CW:(j + 1) * CW], banks[4 + q % 2][:], ACT.Copy).then_inc(a_read, 1)
                    if n == 0 and not first and not last:
                        sigmoid_of_gate(e)
                    if n == 1 and not first and not last:
                        act_rounded(i, e, p)
                if first:
                    gather_read(e + 1)

            all_rounds(act, round_act)
            with more_passes(act) as p:
                all_rounds(act, round_act, p)

        @block.vector
        def _(dve):
            st = Steps(dve, "dve")

            def split_low(n):
                dve.wait_ge(h_ready, n + 1)
                dve.tensor_tensor(wl[n % 8][:], raw[n % 8][:], wh[n % 4][:].bitcast(f32), ALU.subtract) \
                    .then_inc(l_ready, 1)

            def done(ins):
                ins.then_inc(read["dve"], 1)

            def second_norm(t):
                dve.scalar_tensor_tensor(h2[:, t, :], h2[:, t, :], stat[:, 2 * t + 1:2 * t + 2], bc[:, 1, :],
                                         ALU.mult, ALU.add).then_inc(h2_ready, 1)

            def expert_half_split(m, r):
                s, _ = raw_count(m)
                n = NPRE + m
                dve.wait_ge(h_ready, n + 1 + 12 * r)
                dve.tensor_tensor(wl[s][:], raw[s][:], wh[n % 4][:].bitcast(f32), ALU.subtract).then_inc(l_ready, 1)

            def expert_split(q, r):
                for m in (2 * q, 2 * q + 1):
                    expert_half_split(m, r)

            calls = [0]

            def rsqrt(col, n, count, meanwhile=None):
                calls[0] += 1
                var, r, t = stat[:, col:col + n], stat[:, col + n:col + 2 * n], stat[:, 28:28 + n]
                dve.tensor_scalar(var, var, 1.0 / count, EPS, ALU.mult, ALU.add).then_inc(var_ready, 1)
                if meanwhile is not None:
                    st.link(meanwhile())
                dve.wait_ge(std_ready, calls[0])
                st.link(dve.reciprocal(r, r))
                st.link(dve.tensor_tensor(t, r, r, ALU.mult))
                st.link(dve.tensor_tensor(t, t, var, ALU.mult))
                st.link(dve.tensor_scalar(t, t, -0.5, 1.5, ALU.mult, ALU.add))
                st.link(dve.tensor_tensor(r, r, t, ALU.mult))

            st.link(dve.memset(silu_c[:].bitcast(f32), 0.0))
            dve.wait_ge(sigm, 1)
            st.link(dve.tensor_tensor(cc[:].rearrange("p k s -> p s k"), cc[:].rearrange("p k s -> p s k"),
                                      cols_in[:, 0:2, :], ALU.mult))
            st.link(dve.tensor_copy(silu_c[:, :, 0:2], cc[:]))
            dve.tensor_tensor(silu_c[:, :, 2:4], cc[:], silu_c[:, :, 0:2].bitcast(f32), ALU.subtract) \
                .then_inc(silu_ready, 1)
            split_low(0)
            split_low(1)

            def split_h(k):
                dve.wait_ge(h_full, k + 1)
                dve.wait_ge(h_rounded, k + 1)
                dve.tensor_tensor(hL[:, k, CTX:], xT[:, k, CTX:], hH[:, k, CTX:].bitcast(f32), ALU.subtract) \
                    .then_inc(h_split, 1)

            dve.wait_ge(squares, 4)
            rsqrt(0, 4, D)
            for t in range(4):
                dve.tensor_scalar(rows[:, t, :], rows[:, t, :], stat[:, 4 + t:5 + t], None, ALU.mult).then_inc(normed, 1)

            def rope(r, src, table, heads, width, t):
                dst = roped[r % 2]
                n = heads * width
                q = width // 4
                sv = src.rearrange("p (h a s f) -> p h a s f", a=2, s=2, f=q)
                dv = ropes[:, 0:n].rearrange("p (h a s f) -> p h a s f", a=2, s=2, f=q)
                tv = table[:, 1, t - 2, :].rearrange("p (a s f) -> p a s f", s=2, f=q)
                for s_ in range(2):
                    for h in range(heads):
                        ins = dve.tensor_tensor(dv[:, h, :, s_, :], sv[:, h, :, 1 - s_, :], tv[:, :, s_, :], ALU.mult)
                st.link(ins)
                sw = src.rearrange("p (h w) -> p h w", w=width)
                dw = dst[:, 0:n].rearrange("p (h w) -> p h w", w=width)
                cos = table[:, 0, t - 2, :].unsqueeze(1).broadcast_to([P, heads, width])
                last = dve.tensor_tensor(dw, sw, cos, ALU.mult)
                return last, n

            def normalise(h, t):
                u = 2 * h + t
                was_read(dve, ("score", h, t))
                if u:
                    dve.wait_ge(prob_ready, u)
                st.link(dve.reciprocal(stat[:, 21:22], stat[:, 26 + u % 2:27 + u % 2]))
                dve.tensor_scalar(prob[u % 2][:], prob[u % 2][:], stat[:, 21:22], None, ALU.mult).then_inc(prob_ready, 1)

            for n, (name, reader) in enumerate(PLAN):
                if name[0] == "proj":
                    for later, _ in PLAN[n + 1:]:
                        if later[0] == "proj":
                            break
                        if later[0] == "pT":
                            normalise(later[1], later[2])
                for chunk in FIRST_TILE.get(n, []):
                    if chunk + 1 < len(CHUNKS):
                        split_low(2 * chunk + 2)
                        split_low(2 * chunk + 3)
                kind = name[0]
                if kind == "xT" and reader == "dve":
                    full(dve, name)
                    done(dve.tensor_copy(xT[:, name[1], :], bank_of(name)[:]))
                elif kind == "cols":
                    full(dve, name)
                    was_read(dve, ("xT", KB - 2))
                    was_read(dve, ("xT", KB - 1))
                    m = bank_of(name)[:, 0:32].rearrange("p (a k s) -> p a k s", a=2, s=2)
                    st.link(dve.tensor_scalar(scale1[:], m[:, 1], 1.0, None, ALU.add))
                    st.link(dve.tensor_tensor(scale1[:], scale1[:],
                                              cols_in[:, 2, :].unsqueeze(2).broadcast_to([P, KB, 2]), ALU.mult))
                    ins = dve.tensor_copy(shift1[:], m[:, 0])
                    done(ins)
                    was_read(dve, name)
                    for k in range(KB):
                        dve.tensor_scalar(xT[:, k, CTX:], xT[:, k, CTX:], scale1[:, k, 0:1], shift1[:, k, 0:1],
                                          ALU.mult, ALU.add).then_inc(h_full, 1)
                        if k:
                            split_h(k - 1)
                    split_h(KB - 1)
                elif kind == "proj":
                    _, w, c_, t = name
                    if w in ("qa", "ka"):
                        was_read(dve, name)
                        r = ROPED.index(("rT", w, c_, t))
                        if r:
                            in_roped(dve, r - 1)
                        heads = 4 if w == "qa" else 2
                        nn = heads * AD
                        q = roped[r % 2]
                        qv = q[:, 0:nn].rearrange("p (h w) -> p h w", w=AD)
                        if r == 0:
                            dve.wait_ge(in_tables, 80)
                        rsqrt(8, heads, AD)
                        for j in range(heads):
                            ins = dve.scalar_tensor_tensor(qv[:, j, :], qv[:, j, :], stat[:, 8 + heads + j:9 + heads + j],
                                                           gains[:, int(w == "ka"), :], ALU.mult, ALU.mult)
                        if t >= 2:
                            st.link(ins)
                            last, nn = rope(r, q[:, 0:nn], rope_a, heads, AD, t)
                            st.link(last)
                            ins = dve.tensor_tensor(q[:, 0:nn], q[:, 0:nn], ropes[:, 0:nn], ALU.add)
                        ins.then_inc(roped_ready, 1)
                    elif w in ("qr", "kr"):
                        r = ROPED.index(("rT", w, c_, t))
                        in_roped(dve, r - 1)
                        full(dve, ROPED[r - 2])
                        full(dve, name)
                        if t < 2:
                            done(dve.tensor_copy(roped[r % 2][:], bank_of(name)[:]))
                        else:
                            last, nn = rope(r, bank_of(name)[:], rope_r, 2, RQK, t)
                            done(last)
                            was_read(dve, name)
                            dve.tensor_tensor(roped[r % 2][:], roped[r % 2][:], ropes[:], ALU.add).then_inc(roped_ready, 1)
                    elif w == "gr":
                        full(dve, name)
                        dve.wait_ge(sg_ready, 2 * c_ + t - 1)
                        done(dve.tensor_tensor(g[:, t - 2, :], bank_of(name)[:], g[:, t - 2, :], ALU.mult))
                elif kind == "score":
                    _, h, t = name
                    u = 2 * h + t
                    if u:
                        dve.wait_ge(neg_max, u)
                    if u >= 2:
                        was_read(dve, ("score", (u - 2) // 2, (u - 2) % 2))
                    full(dve, name)
                    st.link(dve.tensor_reduce(stat[:, 22:23], bank_of(name)[:], AX.X, ALU.max))
                    dve.tensor_scalar(stat[:, 24 + u % 2:25 + u % 2], stat[:, 22:23], -AD ** -0.5, None, ALU.mult) \
                        .then_inc(neg_max, 1)
                elif kind == "pT":
                    pass
                elif kind == "av":
                    h = name[1]
                    full(dve, name)
                    done(dve.tensor_copy(oaT[:, h, :], bank_of(name)[:, 0:SEQ]))
                elif kind == "rs":
                    _, h, b = name
                    full(dve, name)
                    dve.wait_ge(decay_ready, h + 1)
                    done(dve.scalar_tensor_tensor(decay[:, 2 * b:2 * b + 2, :].rearrange("p a b -> p (a b)"),
                                                  bank_of(name)[:], RQK ** -0.5,
                                                  decay[:, 2 * b:2 * b + 2, :].rearrange("p a b -> p (a b)"),
                                                  ALU.mult, ALU.mult))
                elif kind == "ro" and name[2] == 1:
                    h = name[1]
                    dve.wait_ge(squares, 4 + 2 * h + 2)
                    rsqrt(16, 2, RV)
                    for t in range(2):
                        full(dve, ("ro", h, t))
                        done(dve.scalar_tensor_tensor(g[:, t, :], bank_of(("ro", h, t))[:], stat[:, 18 + t:19 + t],
                                                      g[:, t, :], ALU.mult, ALU.mult))
                elif kind == "ret_o":
                    _, col, t = name
                    full(dve, name)
                    dst = gate_r[:, t - 2, col * CW:(col + 1) * CW]
                    done(dve.tensor_tensor(dst, bank_of(name)[:], dst, ALU.mult))
                elif kind == "attn_o":
                    _, col, t = name
                    full(dve, name)
                    a = gate_a[:, t - 2, col * CW:(col + 1) * CW]
                    y_ = gate_r[:, t - 2, col * CW:(col + 1) * CW]
                    done(dve.tensor_tensor(a, bank_of(name)[:], a, ALU.mult))
                    was_read(dve, name)
                    dve.tensor_tensor(y_, y_, a, ALU.add).then_inc(y_ready, 1)
                elif kind == "yT":
                    j = name[1]
                    dve.wait_ge(yH_ready, j + 1)
                    done(dve.tensor_tensor(yL[:, 2 * j:2 * j + 2, :], bank_of(name)[:].rearrange("p (a b) -> p a b", b=SEQ),
                                           yH[:, 2 * j:2 * j + 2, :].bitcast(f32), ALU.subtract))
                elif kind == "out":
                    _, col, t = name
                    cols = slice(col * CW, (col + 1) * CW)
                    if (col, t) == (0, 2):
                        was_read(dve, ("bc", 1))
                        dve.wait_ge(in_x1, 16)
                    full(dve, name)
                    done(dve.tensor_tensor(h2[:, t - 2, cols], bank_of(name)[:], bc[:, 0, cols], ALU.mult))
                    was_read(dve, name)
                    ins = dve.tensor_tensor(x1[:, t - 2, cols], x1[:, t - 2, cols], h2[:, t - 2, cols], ALU.add)
                    if col == 1:
                        ins.then_inc(x1_ready, 1)
                    else:
                        st.link(ins)
                elif kind == "logits":
                    full(dve, name)
                    dve.wait_ge(in_late, 96)
                    st.link(dve.memset(lp[:], -3.0e38))
                    st.link(dve.memset(rep[:], -3.0e38))
                    lg = bank_of(name)[:, 0:2 * E].rearrange("p (t e) -> p t e", e=E)
                    done(dve.tensor_tensor(lp[:, :, 0:E], lg, br_b[:].unsqueeze(1).broadcast_to([P, 2, E]), ALU.add))
                    was_read(dve, name)
                    for t in range(2):
                        ins = dve.max(out=top[:, t, :], in_=lp[:, t, :])
                        st.link(ins)
                        dve.tensor_scalar(route[:, t:t + 1], top[:, t, 0:1], -1.0, None, ALU.mult).then_inc(neg_top, 1)
                        st.link(dve.tensor_copy(rep[:, t, 0:TOPK], top[:, t, 0:TOPK]))
                        st.link(dve.match_replace(out=lm[:, t, :], in_to_replace=rep[:, t, :], in_values=lp[:, t, :],
                                                  imm_value=-3.2e38))
                    dve.tensor_tensor(chosen[:], lm[:, :, 0:E], lp[:, :, 0:E], ALU.not_equal).then_inc(chosen_ready, 1)
                    dve.wait_ge(chosen_ready, 1)
                    dve.wait_ge(expl, 2)
                    st.link(dve.tensor_tensor(comb[:], comb[:], chosen[:], ALU.mult))
                    st.link(dve.tensor_reduce(route[:, 2:4], comb[:], AX.X, ALU.add))
                    st.link(dve.reciprocal(route[:, 2:4], route[:, 2:4]))
                    dve.tensor_tensor(comb[:], comb[:], route[:, 2:4].unsqueeze(2).broadcast_to([P, 2, E]), ALU.mult) \
                        .then_inc(comb_ready, 1)
                elif kind == "rank":
                    full(dve, name)
                    dve.wait_ge(comb_ready, 1)
                    rk = bank_of(name)[:, 0:2 * E].rearrange("p (t e) -> p t e", e=E)
                    done(dve.scalar_tensor_tensor(rank[:], rk, 1.0, chosen[:], ALU.add, ALU.mult))
                    was_read(dve, name)
                    dve.tensor_scalar(rank[:], rank[:], -1.0, None, ALU.add).then_inc(rank_ready, 1)
                elif kind == "combT":
                    full(dve, name)
                    st.link(dve.tensor_reduce(most[:], bank_of(name)[:, SEQ:SEQ + E], AX.X, ALU.max))
                    dve.tensor_copy(most_int[:], most[:]).then_inc(most_ready, 1)
                    done(dve.tensor_copy(combT[:], bank_of(name)[0:E, 0:SEQ]))
                if name == ("proj", "qa", 1, 3):
                    dve.wait_ge(in_decay, 32)
                    dve.wait_ge(dec_abs, 1)
                    st.link(dve.tensor_scalar(logdec[:], decin[:], 0.0, None, ALU.max))
                    st.link(dve.tensor_tensor(logdec[:], logdec[:], lowdec[:], ALU.add))
                    st.link(dve.tensor_scalar(logdec[:], logdec[:], -1.0, None, ALU.mult))
                    st.link(dve.tensor_scalar(lowdec[:], logdec[:], float(CTX), None, ALU.mult))
                    dve.tensor_scalar(decin[:], logdec[:], -1.0, None, ALU.mult).then_inc(dec_ready, 1)
                if name in (("proj", "gate_a", 1, 3), ("ada", 6)):
                    for j in (0, 1) if kind == "proj" else (2, 3):
                        dve.wait_ge(oH_ready, j + 1)
                        dve.tensor_tensor(oL[:, 4 * j:4 * j + 4, :], oT[:, 4 * j:4 * j + 4, :],
                                          oH[:, 4 * j:4 * j + 4, :].bitcast(f32), ALU.subtract).then_inc(oL_ready, 1)
                if name == ("ret_o", 0, 3):
                    for j in range(2):
                        dve.wait_ge(oH_ready, 5 + j)
                        dve.tensor_tensor(aL[:, 4 * j:4 * j + 4, :], oaT[:, 4 * j:4 * j + 4, :],
                                          aH[:, 4 * j:4 * j + 4, :].bitcast(f32), ALU.subtract).then_inc(oL_ready, 1)
                if name == ("bc", 5):
                    dve.wait_ge(in_norm2, 16)
                    was_read(dve, ("bc", 5))
                    st.link(dve.scalar_tensor_tensor(bc[:, 2, :], bc[:, 2, :], 1.0, norm2_b[:], ALU.add, ALU.mult))
                if name[:2] == ("out", 1):
                    t = name[2] - 2
                    if t:
                        second_norm(0)
                    dve.wait_ge(x1_ready, t + 1)
                    dve.wait_ge(squares, 4 + 2 * RH + t + 1)
                    rsqrt(2 * t, 1, D, lambda: dve.tensor_tensor(h2[:, t, :], x1[:, t, :], bc[:, 2, :], ALU.mult))
                    if t:
                        second_norm(1)
                if name == ("h2T", 3):
                    expert_half_split(0, 0)
                    for t in range(2):
                        dve.wait_ge(h2_rounded, t + 1)
                        dve.tensor_tensor(h2L[:, t, :], h2[:, t, :], h2H[:, t, :].bitcast(f32), ALU.subtract) \
                            .then_inc(h2_split, 1)

            def bias_of(i, block):
                return b1_cols[:, 8 * block:8 * block + 8, bass.ds(i, 1)].broadcast_to([P, 8, CAP])

            def turned_read(i, p):
                e = i + E * p
                dve.wait_ge(t_full, e + 1)
                if not (is_at(i, 0) and is_at(p, FIRST_PASS)):
                    dve.wait_ge(act_low, e)
                for part, (dst, bank) in enumerate(((gate, banks[6]), (up, banks[7]))):
                    dve.tensor_tensor(dst[:].rearrange("p (k c) -> p k c", c=CAP),
                                      bank[:].rearrange("p (k c) -> p k c", c=CAP), bias_of(i, part), ALU.add) \
                        .then_inc(t_read, 1)

            def round_dve(i, p, q0, r):
                e = i + E * p
                first, last = is_at(i, 0), is_at(i, E)
                used = not (is_at(i, 1) and is_at(p, FIRST_PASS))
                if first and not is_at(p, FIRST_PASS):
                    expert_split(0, r)
                if first and is_at(p, FIRST_PASS):
                    expert_half_split(1, r)
                    expert_split(1, r)
                jobs = (4, 5) if last else (0, 1, 2, 3) if first else range(6)
                for n, j in enumerate(jobs):
                    q = q0 + n
                    if is_at(i, E - 1) and n == 5:
                        turned_read(i, p)
                    if not (last and j == 5 or first and n == 0 and is_at(p, FIRST_PASS)):
                        expert_split(q + 1, r)
                    if n == (1 if last else 2) and not first:
                        dve.wait_ge(tp_full, e)
                        if used:
                            dve.wait_ge(scattered, e - 1)
                        dve.tensor_copy(spreadT[:], banks[6][:, 0:SEQ]).then_inc(tp_read, 1)
                    if n == 5 and not is_at(i, E - 1):
                        turned_read(i, p)
                    if j >= 4:
                        dve.wait_ge(g_full, q + 1 + 6 * r)
                        if j == 4 and used:
                            dve.wait_ge(scattered, e - 1)
                        dve.tensor_copy(out2[:, (j - 4) * CW:(j - 3) * CW], banks[4 + q % 2][:]).then_inc(o_read, 1)
                if first:
                    turned_read(i, p)

            all_rounds(dve, round_dve)
            with more_passes(dve) as p:
                all_rounds(dve, round_dve, p)
                dve.wait_ge(scattered, E * p + E)
            for col in range(2):
                cols = slice(col * CW, (col + 1) * CW)
                if col:
                    dve.wait_ge(scattered, E)
                else:
                    dve.wait_ge(half_scattered, 1)
                for t in range(2):
                    part = a_sb[:, (2 * t + col) * CW:(2 * t + col + 1) * CW]
                    ins = dve.tensor_tensor(part, banks[2 * t + col][:], bc[:, 3, cols], ALU.mult)
                st.link(ins)
                for t in range(2):
                    part = a_sb[:, (2 * t + col) * CW:(2 * t + col + 1) * CW]
                    ins = dve.tensor_tensor(x1[:, t, cols], x1[:, t, cols], part, ALU.add)
                ins.then_inc(out_done, 1)

        @block.gpsimd
        def _(pool):
            st = Steps(pool, "pool")
            for k in range(KB):
                pool.wait_ge(hc_rounded, k + 1)
                pool.tensor_tensor(hL[:, k, 0:CTX], xT[:, k, 0:CTX], hH[:, k, 0:CTX].bitcast(f32), ALU.subtract) \
                    .then_inc(hc_split, 1)
            pool.wait_ge(dec_ready, 1)
            for h in range(RH):
                if h:
                    was_read(pool, ("ro", h - 1, 1))
                else:
                    pool.wait_ge(roped_ready, 8)
                    pool.wait_ge(in_tables, 80)
                d2 = decay2[:].rearrange("p (a b) -> p a b", b=SEQ)
                st.link(pool.tensor_scalar(decay[:, 2:4, :], dist[:], 0.0, None, ALU.max))
                st.link(pool.tensor_scalar(decay[:, 2:4, :], decay[:, 2:4, :], logdec[:, h:h + 1], None, ALU.mult))
                st.link(pool.tensor_scalar(d2, dist[:], 0.0, None, ALU.min))
                st.link(pool.tensor_scalar(d2, d2, decin[:, RH + h:RH + h + 1], None, ALU.mult))
                pool.tensor_tensor(decay[:, 2:4, :], decay[:, 2:4, :], d2, ALU.add).then_inc(exponent, 1)
                pool.wait_ge(exp_done, 3 * h + 3)
                pool.tensor_tensor(decay[:, 0:2, :], decay[:, 0:2, :], d2, ALU.add).then_inc(decay_ready, 1)

            full(pool, ("ret_o", 1, 3))
            pool.memset(ones[:], 1.0).then_inc(chain["pool"], 1)
            st.n += 1
            pool.wait_ge(rank_ready, 1)
            pool.wait_ge(in_late, 96)

            def pool_waits(semaphore, value):
                pool.wait_ge(semaphore, value)
                if not isinstance(value, int):
                    pool.nop(nofuse=True)

            def build_onehot(i, e):
                if not is_at(e, 0):
                    pool_waits(onehot_ready, 2 * e)
                pool.tensor_copy(now_rank[:], rank[:, :, bass.ds(i, 1)]).then_inc(columns_ready, 1)
                pool_waits(columns_ready, 3 * e + 1 if is_at(i, 0) else 3 * e - 1)
                for t in range(2):
                    pool.tensor_scalar(onehot[:, t, :], slot_no[:, 0:CAP], now_rank[:, t, :], None,
                                       ALU.is_equal).then_inc(onehot_ready, 1)

            def build_spread(i, e):
                if not is_at(e, 0):
                    pool_waits(spread_ready, 2 * e)
                pool.tensor_copy(own_rank[:], rank[:, :, bass.ds(i, 1)]).then_inc(columns_ready, 1)
                pool.tensor_copy(own_comb[:], comb[:, :, bass.ds(i, 1)]).then_inc(columns_ready, 1)
                pool_waits(columns_ready, 3 * e + 3 if is_at(i, E - 1) else 3 * e + 4)
                for t in range(2):
                    pool.tensor_scalar(spread[:, t, :], slot_no[:], own_rank[:, t, :],
                                       own_comb[:, t, :], ALU.is_equal, ALU.mult).then_inc(spread_ready, 1)

            def round_pool(i, p, q0, r):
                e = i + E * p
                first = is_at(i, 0)
                if is_at(i, E):
                    return
                if first:
                    if not is_at(p, FIRST_PASS):
                        pool_waits(spread_ready, 2 * e)
                        pool_waits(onehot_ready, 2 * e)
                        pool.tensor_scalar(rank[:], rank[:], -float(CAP), None, ALU.add).then_inc(shifted, 1)
                        pool_waits(shifted, p)
                    build_onehot(i, e)
                if not is_at(i, E - 1):
                    pool_waits(x_full, e + 1)
                    build_onehot(i + 1, e + 1)
                if not (first and is_at(p, FIRST_PASS)):
                    pool_waits(tp_full, e)
                build_spread(i, e)
                pool_waits(t_read, 2 * e + 2)
                pool.tensor_scalar(gate[:], gate[:], LIMIT, None, ALU.min).then_inc(clipped, 1)
                pool.tensor_scalar(up[:], up[:], LIMIT + 1.0, 1.0 - LIMIT, ALU.min, ALU.max).then_inc(up_steps, 1)
                pool_waits(clipped, e + 1)
                pool_waits(up_steps, 2 * e + 1)
                pool.tensor_tensor(up[:], up[:], gate[:], ALU.mult).then_inc(up_steps, 1)
                pool_waits(up_steps, 2 * e + 2)
                pool_waits(sig_ready, e + 1)
                pool.tensor_tensor(gate[:], up[:], sig[:], ALU.mult).then_inc(act_ready, 1)
                pool_waits(act_high, e + 1)
                pool.tensor_tensor(act_hl[:, :, CAP:2 * CAP], gate[:].rearrange("p (k c) -> p k c", c=CAP),
                                   act_hl[:, :, 0:CAP].bitcast(f32), ALU.subtract).then_inc(act_low, 1)

            all_rounds(pool, round_pool)
            with more_passes(pool) as p:
                all_rounds(pool, round_pool, p)

        @block.tensor
        def _(pe):
            def tile(name, emit, signal=True):
                n = TILE_AT[name]
                if n >= 8:
                    was_read(pe, PLAN[n - 8][0])
                last = emit(banks[n % 8])
                if signal:
                    last.then_inc(psum_full, 1)
                return last

            def halves(n):
                pe.wait_ge(l_ready, n + 1)

            def three(ps, hi, lo, n, k, start, stop):
                wslot, lslot, kk = (2 * n + k // 4) % 4, (2 * n + k // 4) % 8, k % 4
                pe.matmul(ps[:], hi, wh[wslot][:, kk, :], start=start, stop=False)
                pe.matmul(ps[:], hi, wl[lslot][:, kk, :], start=False, stop=False)
                return pe.matmul(ps[:], lo, wh[wslot][:, kk, :], start=False, stop=stop)

            def product(ps, hi, lo, n, cols, k0=0, start=True, stop=True, blocks_of=None):
                for k in range(KB):
                    if k % 4 == 0:
                        halves(2 * n + k // 4)
                    if blocks_of is not None and (k0 + k) % blocks_of[2] == 0:
                        pe.wait_ge(blocks_of[0], blocks_of[1] + (k0 + k) // blocks_of[2] + 1)
                    last = three(ps, hi[:, k0 + k, cols], lo[:, k0 + k, cols], n, k, start and k == 0, stop and k == KB - 1)
                return last

            def turn(ps, parts):
                for j, src in enumerate(parts):
                    last = pe.transpose(ps[0:src.shape[1], j * src.shape[0]:(j + 1) * src.shape[0]], src,
                                        ident[0:src.shape[0], 0:src.shape[0]])
                return last

            pe.wait_ge(in_ident, 32)
            for n, (name, reader) in enumerate(PLAN):
                kind = name[0]
                if kind == "xT":
                    k = name[1]
                    if k == 0:
                        pe.wait_ge(normed, 4)
                    tile(name, lambda ps: turn(ps, [rows[:, t, k * P:(k + 1) * P] for t in range(4)]))
                elif kind == "ada":
                    ch = CHUNK_OF[name]
                    if name[1] == 0:
                        pe.wait_ge(silu_ready, 1)

                    def emit(ps):
                        for k in range(KB):
                            if k % 4 == 0:
                                halves(2 * ch + k // 4)
                            ws, ls = (2 * ch + k // 4) % 4, (2 * ch + k // 4) % 8
                            pe.matmul(ps[:], silu_c[:, k, :], wh[ws][:, k % 4, :], start=k == 0, stop=False)
                            last = pe.matmul(ps[:], silu_c[:, k, :], wl[ls][:, k % 4, :], start=False, stop=k == KB - 1)
                        return last
                    tile(name, emit)
                elif kind == "cols":
                    was_read(pe, ("ada", 3))
                    pe.wait_ge(in_bada, 16)

                    def emit(ps):
                        for b in range(16):
                            last = pe.matmul(ps[:, 2 * b:2 * b + 2], mod1[:, b * P:(b + 1) * P], sel[:, 0:2],
                                             start=True, stop=True)
                        return last
                    tile(name, emit)
                elif kind == "proj":
                    _, w, c_, t = name
                    if name == ("proj", "ka", 0, 0):
                        pe.wait_ge(hc_split, KB)
                    tile(name, lambda ps: product(ps, hH, hL, CHUNK_OF[(w, c_)], slice(t * P, (t + 1) * P),
                                                  blocks_of=(h_split, 0, 1) if name == ("proj", "qa", 0, 2) else None))
                elif kind == "rT":
                    r = ROPED.index(name)
                    in_roped(pe, r)
                    blocks = 2 if name[1] == "ka" else 4
                    tile(name, lambda ps: turn(ps, [roped[r % 2][:, b * P:(b + 1) * P] for b in range(blocks)]))
                elif kind == "score":
                    _, h, t = name
                    if h == 0:
                        was_read(pe, ("rT", "ka", 0, 3))
                    tile(name, lambda ps: pe.matmul(ps[:], qaT[:, h, t * P:(t + 1) * P], kaT[:, h // (AH // AKV), :],
                                                    start=True, stop=True))
                elif kind == "pT":
                    _, h, t = name
                    pe.wait_ge(prob_ready, 2 * h + t + 1)
                    tile(name, lambda ps: turn(ps, [prob[t][:, b * P:(b + 1) * P] for b in range(4)]))
                elif kind == "av":
                    h = name[1]
                    kv = h // (AH // AKV)
                    was_read(pe, ("pT", h, 1))

                    def emit(ps):
                        for b in range(4):
                            last = pe.matmul(ps[:, 0:SEQ], va[:, b, kv * AD:(kv + 1) * AD], probT[:, b, :],
                                             start=b == 0, stop=b == 3)
                        return last
                    tile(name, emit)
                elif kind == "rs":
                    _, h, b = name
                    hh = h % 2
                    was_read(pe, ("rT", "kr", h // 2, 3))

                    def emit(ps):
                        for m in range(2):
                            for k in range(2):
                                last = pe.matmul(ps[:, m * SEQ:(m + 1) * SEQ],
                                                 krT[:, 2 * hh + k, (2 * b + m) * P:(2 * b + m + 1) * P],
                                                 qrT[:, 2 * hh + k, :], start=k == 0, stop=k == 1)
                        return last
                    tile(name, emit)
                elif kind == "ro":
                    _, h, t = name
                    was_read(pe, ("rs", h, 1))
                    was_read(pe, ("proj", "vr", h, 3))

                    def emit(ps):
                        for m in range(4):
                            last = pe.matmul(ps[:], decay[:, m, t * P:(t + 1) * P], v[:, m, :], start=m == 0, stop=m == 3)
                        return last
                    tile(name, emit)
                elif kind == "oT":
                    _, h, b = name
                    was_read(pe, ("ro", h, 1))
                    tile(name, lambda ps: turn(ps, [g[:, t, (2 * b + j) * P:(2 * b + j + 1) * P]
                                                    for j in range(2) for t in range(2)]))
                elif kind == "b1":
                    pe.wait_ge(in_b1, 16)
                    tile(name, lambda ps: turn(ps, [b1_rows[:, b * P:(b + 1) * P] for b in range(16)]))
                elif kind == "ret_o":
                    _, col, t = name
                    if t == 3:
                        continue
                    for kh in range(2):
                        for t_ in (2, 3):
                            nm = ("ret_o", col, t_)
                            cols = slice((t_ - 2) * P, (t_ - 1) * P)

                            def emit(ps):
                                return product(ps, oH, oL, CHUNK_OF[("ret_o", 2 * col + kh)], cols, k0=KB * kh,
                                               start=kh == 0, stop=kh == 1,
                                               blocks_of=(oL_ready, 0, 4) if (col, t_) == (0, 2) else None)
                            if kh == 0:
                                last = tile(nm, emit, signal=False)
                                if t_ == 3:
                                    last.then_inc(half_k_used, 1)
                            else:
                                emit(bank_of(nm)).then_inc(psum_full, 1)
                elif kind == "attn_o":
                    _, c_, t = name
                    tile(name, lambda ps: product(ps, aH, aL, CHUNK_OF[("attn_o", c_)], slice((t - 2) * P, (t - 1) * P),
                                                  blocks_of=(oL_ready, 4, 4) if (c_, t) == (0, 2) else None))
                elif kind == "yT":
                    j = name[1]
                    pe.wait_ge(y_ready, 2 if j < 2 else 4)
                    tile(name, lambda ps: turn(ps, [gate_r[:, t, (2 * j + k) * P:(2 * j + k + 1) * P]
                                                    for k in range(2) for t in range(2)]))
                elif kind == "bc":
                    j = name[1]
                    if j == 0:
                        was_read(pe, ("ada", 9))
                        pe.wait_ge(in_mod2, 16)
                    if j == 6:
                        was_read(pe, ("ada", 10))
                        pe.wait_ge(in_late, 96)
                    src = mod2[:, j * CW:(j + 1) * CW] if j < 6 else mod_g2[:, (j - 6) * CW:(j - 5) * CW]
                    tile(name, lambda ps: pe.matmul(ps[:], sel[:, 2:2 + P], src,
                                                    start=True, stop=True))
                elif kind == "out":
                    _, c_, t = name
                    if name == ("out", 0, 2):
                        was_read(pe, ("yT", 3))
                    tile(name, lambda ps: product(ps, yH, yL, CHUNK_OF[("out", c_)], slice((t - 2) * P, (t - 1) * P)))
                elif kind == "h2T":
                    j = name[1]
                    pe.wait_ge(h2_ready, 2)
                    tile(name, lambda ps: turn(ps, [h2[:, t, (2 * j + k) * P:(2 * j + k + 1) * P]
                                                    for k in range(2) for t in range(2)]))
                elif kind == "logits":
                    pe.wait_ge(in_late, 96)

                    def emit(ps):
                        for t in range(2):
                            for k in range(KB):
                                if t == 0 and k % 2 == 0:
                                    was_read(pe, ("h2T", k // 2))
                                last = pe.matmul(ps[:, t * E:(t + 1) * E], h2T[:, k, t * P:(t + 1) * P], wr_sb[:, k, :],
                                                 start=k == 0, stop=k == KB - 1)
                        return last
                    tile(name, emit)
                elif kind == "rank":
                    pe.wait_ge(chosen_ready, 1)
                    pe.wait_ge(chain["pool"], 5 * RH + 1 - RH)

                    def emit(ps):
                        pe.matmul(ps[:, 0:E], tri[:], chosen[:, 0, :], start=True, stop=True)
                        pe.matmul(ps[:, E:2 * E], ones[:], chosen[:, 0, :], start=True, stop=False)
                        return pe.matmul(ps[:, E:2 * E], tri[:], chosen[:, 1, :], start=False, stop=True)
                    tile(name, emit)
                elif kind == "combT":
                    pe.wait_ge(comb_ready, 1)

                    def emit(ps):
                        turn(ps, [comb[:, t, :] for t in range(2)])
                        pe.matmul(ps[:, SEQ:SEQ + E], ones[:], chosen[:, 0, :], start=True, stop=False)
                        return pe.matmul(ps[:, SEQ:SEQ + E], ones[:], chosen[:, 1, :], start=False, stop=True)
                    tile(name, emit)

            def output_bias():
                was_read(pe, ("combT",))
                pe.wait_ge(in_b2, 16)
                for t in range(2):
                    for col in range(2):
                        pe.matmul(banks[2 * t + col][:], combT[:, t * P:(t + 1) * P], b2_sb[:, col * CW:(col + 1) * CW],
                                  start=True, stop=False, skip_group_check=True)

            def gather(e):
                pe.wait_ge(onehot_ready, 2 * e + 2)
                for k in range(KB):
                    for part, rows_ in enumerate((h2H, h2L)):
                        cols = slice((k % 4) * P + part * CAP, (k % 4) * P + (part + 1) * CAP)
                        for t in range(2):
                            last = pe.matmul(banks[6 + k // 4][:, cols], rows_[:, t, k * P:(k + 1) * P],
                                             onehot[:, t, :], start=t == 0, stop=t == 1)
                last.then_inc(x_full, 1)

            def weights_times(ps, lhs, q, r):
                for k in range(KB):
                    m = 2 * q + k // 4
                    n = NPRE + m
                    if k % 4 == 0:
                        pe.wait_ge(l_ready, n + 1 + 12 * r)
                    pe.matmul(ps[:], lhs[:, k, :], wh[n % 4][:, k % 4, :], start=k == 0, stop=False)
                    last = pe.matmul(ps[:], lhs[:, k, :], wl[raw_count(m)[0]][:, k % 4, :],
                                     start=False, stop=k == KB - 1)
                    if k == 3:
                        last.then_inc(first_half_used, 1)
                last.then_inc(g_full, 1)

            def turn_first(e, i):
                pe.wait_ge(a_read, 4 * e + 4)
                if is_at(i, E - 1):
                    pe.wait_ge(tp_read, e)
                else:
                    pe.wait_ge(xg_ready, 2 * e + 4)
                for b in range(16):
                    ins = pe.matmul(banks[6 + b // 8][:, (b % 8) * CAP:(b % 8 + 1) * CAP],
                                    a_sb[:, b * P:(b + 1) * P], ident2[:], start=True, stop=True)
                ins.then_inc(t_full, 1)

            def scatter(e, stop=False):
                pe.wait_ge(tp_read, e + 1)
                for col in range(2):
                    pe.wait_ge(o_read, 2 * e + 1 + col)
                    for t in range(2):
                        ins = pe.matmul(banks[2 * t + col][:], spreadT[:, t * P:(t + 1) * P],
                                        out2[:, col * CW:(col + 1) * CW], start=False, stop=stop,
                                        skip_group_check=True)
                    if stop and col == 0:
                        ins.then_inc(half_scattered, 1)
                ins.then_inc(scattered, 1)

            def round_pe(i, p, q0, r):
                e = i + E * p
                first, last = is_at(i, 0), is_at(i, E)
                begun = not (first and is_at(p, FIRST_PASS))
                if first:
                    if begun:
                        pe.wait_ge(tp_read, e)
                    gather(e)
                if last:
                    scatter(e - 2)
                jobs = (4, 5) if last else (0, 1, 2, 3) if first else range(6)
                for n, j in enumerate(jobs):
                    q = q0 + n
                    if last:
                        pe.wait_ge(o_read, 2 * (e - 2) + 1 + n)
                    elif j >= 2:
                        pe.wait_ge(a_read, 4 * e + j - 1)
                    elif is_at(i, 1):
                        pe.wait_ge(a_read, 4 * (e - 1) + 3 + j)
                    elif begun:
                        pe.wait_ge(o_read, (2 * e if first else 2 * (e - 1)) - 1 + j)
                    if j == 0:
                        pe.wait_ge(xg_ready, 2 * e + 2)
                    if j == 4:
                        pe.wait_ge(act_low, e)
                    weights_times(banks[4 + q % 2], xg if j < 4 else act_hl, q, r)
                    if n == 0 and first and not begun:
                        output_bias()
                    if n == 0 and not first and not last and not is_at(i, 1):
                        scatter(e - 2)
                    if n == 1 and not first:
                        pe.wait_ge(spread_ready, 2 * e)
                        pe.wait_ge(t_read, 2 * e)
                        for t in range(2):
                            ins = pe.transpose(banks[6][:, t * P:(t + 1) * P], spread[:, t, :], ident[:])
                        ins.then_inc(tp_full, 1)
                    if j == 3 and not is_at(i, E - 1):
                        if not first:
                            pe.wait_ge(tp_read, e)
                        pe.wait_ge(xg_ready, 2 * e + 2)
                        gather(e + 1)
                    if j == 4 and not last:
                        turn_first(e, i)
                if first:
                    turn_first(e, i)
                if last:
                    scatter(e - 1, stop=True)

            for reader_ in ("act", "dve"):
                pe.wait_ge(read[reader_], sum(w == reader_ for _, w in PLAN))
            all_rounds(pe, round_pe)
            with more_passes(pe) as p:
                all_rounds(pe, round_pe, p)


def constants():
    import numpy as np

    m = np.zeros((P, C_END), np.float32)
    m[:, C_ID:C_ID + P] = np.eye(P)
    m[:, C_ID2:C_ID2 + CAP] = np.tile(np.eye(CAP), (2, 1))
    m[:, C_SLOT:C_SLOT + P] = np.arange(P) % CAP
    m[:, C_TRI:C_TRI + P] = np.triu(np.ones((P, P)), 1)
    row = np.arange(P)[:, None]
    for t in range(2):
        m[:, C_DIST + t * SEQ:C_DIST + (t + 1) * SEQ] = np.arange(SEQ)[None, :] - (row + t * P)
    m[0:5, C_SEL] = (1, 0, 1, 0, 1)
    m[0:5, C_SEL + 1] = (0, 1, 0, 1, 1)
    m[0:5, C_SEL + 2:C_SEL + 2 + P] = np.array([1, 0, 1, 0, 1])[:, None]
    for at, width in ((C_ROPER, RQK), (C_ROPEA, AD)):
        n = width // 4
        freq = (np.float32(10000.0) ** (-np.arange(n, dtype=np.float32) / np.float32(n))).astype(np.float32)
        for t in range(2):
            tok = np.arange(P) + t * P
            for axis, pos in enumerate((tok // 64, tok % 64)):
                ang = pos.astype(np.float32)[:, None] * freq
                for half in range(2):
                    o = at + t * width + (2 * axis + half) * n
                    m[:, o:o + n] = np.cos(ang)
                    m[:, o + 2 * width:o + 2 * width + n] = np.sin(ang) * (1 if half else -1)
    return m


_INS = ["x", "ctx", "norm2", "w_ada", "b_ada", "w_in", "ret_decay_f", "ret_decay_b", "attn_q_norm", "attn_k_norm",
        "w_ret_o", "w_attn_o", "w_out", "w_router", "b_router", "w_exp_in", "b_exp_in", "w_exp_out", "b_exp_out"]


def lay_out(inputs):
    import numpy as np

    arrays = {f"in_{name}": np.ascontiguousarray(inputs[name]) for name in _INS}
    columns = [np.asarray(inputs[name]).reshape(KB, P).T for name in ("c", "c_ctx", "norm1")]
    arrays["in_vectors"] = np.ascontiguousarray(np.concatenate(columns, axis=1))
    arrays["in_consts"] = constants()
    return arrays


def kernel(**inputs):
    import numpy as np
    import concourse.bacc as bacc
    from concourse.bass_utils import run_bass_kernel_spmd

    nc = bacc.Bacc("TRN2", target_bir_lowering=False, num_devices=1)
    arrays, args = lay_out(inputs), []
    for name, a in arrays.items():
        args.append(nc.dram_tensor(name, a.shape, mybir.dt.from_np(a.dtype), kind="ExternalInput").ap())
    args.append(nc.dram_tensor("out_0", (1, SEQ, D), mybir.dt.float32, kind="ExternalOutput").ap())
    hybrid_block(nc, *args)
    r = run_bass_kernel_spmd(nc, [arrays], core_ids=[0])
    return np.asarray(r.results[0]["out_0"])
```
